# Optimizing a Trainium2 kernel written in Bass

```python
import jax, jax.numpy as jnp
from jax import lax
import numpy as np
import math

D_MODEL = 1024
BATCH = 1
SEQ = 256
DEPTH = 2

N_HEADS = 8
N_KV_HEADS = 2
HEAD_DIM = 64
GQA_GROUP = N_HEADS // N_KV_HEADS
ATTN_WIDTH = N_HEADS * HEAD_DIM
KV_WIDTH = N_KV_HEADS * HEAD_DIM
WINDOW = 128
BLOCK = 128
ROPE_THETA = 500000.0
ROT_DIM = HEAD_DIM // 4
POOL_SIZES = (2, 4, 8, 16)
POOL_WIDTH = D_MODEL // 2
POOL_GROUP = POOL_WIDTH // len(POOL_SIZES)
N_BRANCHES = 2
IN_WIDTH = ATTN_WIDTH + 2 * KV_WIDTH + POOL_WIDTH + N_BRANCHES * D_MODEL
D_FF = 2816
EPS = 1e-6


def rms_norm(x, g):
    x32 = x.astype(jnp.float32)
    y = x32 * lax.rsqrt(jnp.mean(x32 * x32, axis=-1, keepdims=True) + EPS)
    return (y * g.astype(jnp.float32)).astype(x.dtype)

def swiglu(u, w1, w3, w2):
    return (jax.nn.silu(u @ w1) * (u @ w3)) @ w2

def rope_tables(s):
    inv_freq = 1.0 / (ROPE_THETA ** (jnp.arange(0, ROT_DIM, 2, dtype=jnp.float32) / ROT_DIM))
    ang = jnp.arange(s, dtype=jnp.float32)[:, None] * inv_freq[None, :]
    return jnp.cos(ang), jnp.sin(ang)

def partial_rope(t, cos, sin):
    half = ROT_DIM // 2
    t32 = t.astype(jnp.float32)
    t1 = t32[..., :half]
    t2 = t32[..., half:ROT_DIM]
    c = cos[None, :, None, :]
    s = sin[None, :, None, :]
    rot = jnp.concatenate([t1 * c - t2 * s, t2 * c + t1 * s, t32[..., ROT_DIM:]], axis=-1)
    return rot.astype(t.dtype)

def banded_blocks(t):
    b, s = t.shape[0], t.shape[1]
    nb = s // BLOCK
    tp = jnp.pad(t, ((0, 0), (BLOCK, BLOCK), (0, 0), (0, 0)))
    parts = [tp[:, i * BLOCK:i * BLOCK + s].reshape(b, nb, BLOCK, t.shape[2], t.shape[3]) for i in range(3)]
    return jnp.concatenate(parts, axis=2)

def windowed_gqa(q, k, v, sink):
    b, s = q.shape[0], q.shape[1]
    nb = s // BLOCK
    qb = q.reshape(b, nb, BLOCK, N_KV_HEADS, GQA_GROUP, HEAD_DIM)
    kb = banded_blocks(k)
    vb = banded_blocks(v)
    scores = jnp.einsum('bnqhgd,bnkhd->bhgnqk', qb, kb).astype(jnp.float32) * (HEAD_DIM ** -0.5)
    blk = jnp.arange(nb)[:, None, None]
    qpos = blk * BLOCK + jnp.arange(BLOCK)[None, :, None]
    kpos = blk * BLOCK - BLOCK + jnp.arange(3 * BLOCK)[None, None, :]
    valid = (jnp.abs(qpos - kpos) <= WINDOW) & (kpos >= 0) & (kpos < s)
    scores = jnp.where(valid, scores, -1e30)
    sink_logit = jnp.broadcast_to(
        sink.astype(jnp.float32).reshape(1, N_KV_HEADS, GQA_GROUP, 1, 1, 1), scores.shape[:-1] + (1,))
    probs = jax.nn.softmax(jnp.concatenate([scores, sink_logit], axis=-1), axis=-1)[..., :-1]
    out = jnp.einsum('bhgnqk,bnkhd->bnqhgd', probs.astype(v.dtype), vb)
    return out.reshape(b, s, ATTN_WIDTH)

def multiscale_pool(p, pool_w, pool_scale):
    b, s, _ = p.shape
    p32 = p.astype(jnp.float32)
    cs = jnp.concatenate([jnp.zeros((b, 1, POOL_WIDTH), jnp.float32), jnp.cumsum(p32, axis=1)], axis=1)
    t = jnp.arange(s)
    outs = []
    for gi, w in enumerate(POOL_SIZES):
        sl = slice(gi * POOL_GROUP, (gi + 1) * POOL_GROUP)
        lo = jnp.clip(t - w // 2, 0, s)
        hi = jnp.clip(t + w // 2, 0, s)
        cnt = (hi - lo).astype(jnp.float32)[None, :, None]
        csg = cs[..., sl]
        mean = (jnp.take(csg, hi, axis=1) - jnp.take(csg, lo, axis=1)) / cnt
        outs.append(mean - p32[..., sl])
    pooled = jnp.stack(outs, axis=2).astype(p.dtype)
    mixed = jnp.einsum('bsgc,gcd->bsgd', pooled, pool_w).reshape(b, s, POOL_WIDTH)
    return mixed * pool_scale

def token_mixer(u, w_in, b_gate, attn_sink, pool_w, pool_scale, w_br_attn, w_br_pool, w_out, cos, sin):
    b, s, _ = u.shape
    proj = u @ w_in
    splits = np.cumsum([ATTN_WIDTH, KV_WIDTH, KV_WIDTH, POOL_WIDTH, D_MODEL]).tolist()
    q, k, v, p, ga, gb = jnp.split(proj, splits, axis=-1)
    q = partial_rope(q.reshape(b, s, N_HEADS, HEAD_DIM), cos, sin)
    k = partial_rope(k.reshape(b, s, N_KV_HEADS, HEAD_DIM), cos, sin)
    v = v.reshape(b, s, N_KV_HEADS, HEAD_DIM)
    y_attn = windowed_gqa(q, k, v, attn_sink) @ w_br_attn
    y_pool = multiscale_pool(p, pool_w, pool_scale) @ w_br_pool
    gate_a = jax.nn.sigmoid(ga + b_gate[:D_MODEL])
    gate_b = jax.nn.sigmoid(gb + b_gate[D_MODEL:])
    return (gate_a * y_attn + gate_b * y_pool) @ w_out

def _w(key, shape, fan_in):
    return jax.random.normal(key, shape, jnp.float32) * (fan_in ** -0.5)

def _gain(key, shape):
    return 1.0 + 0.05 * jax.random.normal(key, shape, jnp.float32)

def first_inputs(seed: int = 0) -> dict:
    key = jax.random.key(seed)
    ks = jax.random.split(key, 22)
    L = DEPTH
    return {
        "x": jax.random.normal(ks[0], (BATCH, SEQ, D_MODEL), jnp.float32),
        "ffn1_norm": _gain(ks[1], (L, D_MODEL)),
        "ffn1_w1": _w(ks[2], (L, D_MODEL, D_FF), D_MODEL),
        "ffn1_w3": _w(ks[3], (L, D_MODEL, D_FF), D_MODEL),
        "ffn1_w2": _w(ks[4], (L, D_FF, D_MODEL), D_FF),
        "mix_norm": _gain(ks[5], (L, D_MODEL)),
        "w_in": _w(ks[6], (L, D_MODEL, IN_WIDTH), D_MODEL),
        "b_gate": 0.02 * jax.random.normal(ks[7], (L, N_BRANCHES * D_MODEL), jnp.float32),
        "attn_sink": 0.5 * jax.random.normal(ks[8], (L, N_HEADS), jnp.float32),
        "pool_w": _w(ks[9], (L, len(POOL_SIZES), POOL_GROUP, POOL_GROUP), POOL_GROUP),
        "pool_scale": _gain(ks[10], (L, POOL_WIDTH)),
        "w_branch_attn": _w(ks[11], (L, ATTN_WIDTH, D_MODEL), ATTN_WIDTH),
        "w_branch_pool": _w(ks[12], (L, POOL_WIDTH, D_MODEL), POOL_WIDTH),
        "w_out": _w(ks[13], (L, D_MODEL, D_MODEL), D_MODEL),
        "ffn2_norm": _gain(ks[14], (L, D_MODEL)),
        "ffn2_w1": _w(ks[15], (L, D_MODEL, D_FF), D_MODEL),
        "ffn2_w3": _w(ks[16], (L, D_MODEL, D_FF), D_MODEL),
        "ffn2_w2": _w(ks[17], (L, D_FF, D_MODEL), D_FF),
        "final_norm": _gain(ks[18], (D_MODEL,)),
    }

def first_block(x, ffn1_norm, ffn1_w1, ffn1_w3, ffn1_w2, mix_norm, w_in, b_gate, attn_sink, pool_w,
              pool_scale, w_branch_attn, w_branch_pool, w_out, ffn2_norm, ffn2_w1, ffn2_w3, ffn2_w2,
              final_norm):
    cos, sin = rope_tables(x.shape[1])
    h = x
    for l in range(DEPTH):
        h = h + 0.5 * swiglu(rms_norm(h, ffn1_norm[l]), ffn1_w1[l], ffn1_w3[l], ffn1_w2[l])
        h = h + token_mixer(rms_norm(h, mix_norm[l]), w_in[l], b_gate[l], attn_sink[l], pool_w[l],
                            pool_scale[l], w_branch_attn[l], w_branch_pool[l], w_out[l], cos, sin)
        h = h + 0.5 * swiglu(rms_norm(h, ffn2_norm[l]), ffn2_w1[l], ffn2_w3[l], ffn2_w2[l])
    return rms_norm(h, final_norm)


SSD_D_INNER = D_MODEL
SSD_HEADDIM = 64
SSD_HEADS = SSD_D_INNER // SSD_HEADDIM
SSD_GROUPS = 2
SSD_HPG = SSD_HEADS // SSD_GROUPS
SSD_STATE = 128
SSD_CONV = 4
SSD_CHUNK = 128
SSD_CONV_DIM = SSD_D_INNER + 2 * SSD_GROUPS * SSD_STATE
RET_HEADS = 4
RET_QK_DIM = 128
RET_HEAD_V = D_MODEL // RET_HEADS
RET_CHUNK = 128
ROPE_BASE = 10000.0
ATT_Q_HEADS = 16
ATT_KV_HEADS = 2
ATT_GROUP = ATT_Q_HEADS // ATT_KV_HEADS
ATT_HEAD_DIM = D_MODEL // ATT_Q_HEADS
ATT_BLOCK = 128
REL_BUCKETS = 32
REL_MAX_EXACT = REL_BUCKETS // 2
REL_MAX_DIST = 128
N_BRANCH = 3
BRANCH_WIDTH = D_MODEL
NEG = -1e30

IN_SPLIT_SIZES = (
    SSD_D_INNER,
    SSD_CONV_DIM,
    SSD_HEADS,
    RET_HEADS * RET_QK_DIM,
    RET_HEADS * RET_QK_DIM,
    RET_HEADS * RET_HEAD_V,
    RET_HEADS * RET_HEAD_V,
    ATT_Q_HEADS * ATT_HEAD_DIM,
    ATT_KV_HEADS * ATT_HEAD_DIM,
    ATT_KV_HEADS * ATT_HEAD_DIM,
    N_BRANCH * D_MODEL,
)
IN_WIDTH_2 = sum(IN_SPLIT_SIZES)


def rmsnorm(x, g):
    xf = x.astype(jnp.float32)
    y = xf * lax.rsqrt(jnp.mean(xf * xf, axis=-1, keepdims=True) + EPS)
    return (y * g.astype(jnp.float32)).astype(x.dtype)

def swiglu_2(x, w_in, w_out):
    a, b = jnp.split(x @ w_in, 2, axis=-1)
    return (jax.nn.silu(a) * b) @ w_out

def causal_dwconv(x, w, b):
    c = x.shape[-1]
    y = lax.conv_general_dilated(x, w[:, None, :].astype(x.dtype), (1,), [(SSD_CONV - 1, 0)],
                                 dimension_numbers=('NWC', 'WIO', 'NWC'), feature_group_count=c)
    return y + b

def ssd_mixer(z, xbc, dt_raw, conv_w, conv_b, dt_bias, a_log, d_skip, norm_g):
    bsz, L, _ = z.shape
    nc = L // SSD_CHUNK
    xbc = jax.nn.silu(causal_dwconv(xbc, conv_w, conv_b))
    xs, bm, cm = jnp.split(xbc, [SSD_D_INNER, SSD_D_INNER + SSD_GROUPS * SSD_STATE], axis=-1)
    xs = xs.reshape(bsz, nc, SSD_CHUNK, SSD_GROUPS, SSD_HPG, SSD_HEADDIM)
    bm = bm.reshape(bsz, nc, SSD_CHUNK, SSD_GROUPS, SSD_STATE)
    cm = cm.reshape(bsz, nc, SSD_CHUNK, SSD_GROUPS, SSD_STATE)
    dt = jax.nn.softplus(dt_raw.astype(jnp.float32) + dt_bias.astype(jnp.float32))
    dt = dt.reshape(bsz, nc, SSD_CHUNK, SSD_GROUPS, SSD_HPG)
    a = -jnp.exp(a_log.astype(jnp.float32)).reshape(SSD_GROUPS, SSD_HPG)
    da = jnp.moveaxis(dt * a, 2, -1)
    a_cs = jnp.cumsum(da, axis=-1)
    causal = jnp.tril(jnp.ones((SSD_CHUNK, SSD_CHUNK), dtype=bool))
    seg = a_cs[..., :, None] - a_cs[..., None, :]
    lmat = jnp.exp(jnp.where(causal, seg, -jnp.inf))
    xdt = xs * dt[..., None]
    cb = jnp.einsum('bclgn,bcsgn->bcgls', cm, bm)
    y_diag = jnp.einsum('bcgjls,bcsgjp->bclgjp', cb[:, :, :, None] * lmat, xdt)
    decay_st = jnp.moveaxis(jnp.exp(a_cs[..., -1:] - a_cs), -1, 2)
    states = jnp.einsum('bclgn,bclgjp->bcgjpn', bm, xdt * decay_st[..., None])
    chunk_decay = jnp.exp(a_cs[..., -1])

    def step(h, inp):
        s, dcy = inp
        return (h * dcy[..., None, None] + s).astype(h.dtype), h

    h0 = jnp.zeros_like(states[:, 0])
    _, prev = lax.scan(step, h0, (jnp.moveaxis(states, 1, 0), jnp.moveaxis(chunk_decay, 1, 0)))
    prev = jnp.moveaxis(prev, 0, 1)
    decay_out = jnp.moveaxis(jnp.exp(a_cs), -1, 2)
    y_off = jnp.einsum('bclgn,bcgjpn->bclgjp', cm, prev) * decay_out[..., None]
    y = y_diag + y_off + xs * d_skip.reshape(SSD_GROUPS, SSD_HPG, 1)
    y = y.reshape(bsz, L, SSD_D_INNER).astype(z.dtype)
    return rmsnorm(y * jax.nn.silu(z), norm_g)

def rope(x, cos, sin):
    x1, x2 = jnp.split(x, 2, axis=-1)
    c = cos[:, None, :]
    s = sin[:, None, :]
    return jnp.concatenate([x1 * c - x2 * s, x2 * c + x1 * s], axis=-1)

def retention_mixer(q, k, v, g, gn_g, cos, sin):
    bsz, L, _ = q.shape
    nc = L // RET_CHUNK
    q = rope(q.reshape(bsz, L, RET_HEADS, RET_QK_DIM), cos, sin)
    k = rope(k.reshape(bsz, L, RET_HEADS, RET_QK_DIM), cos, sin) * (RET_QK_DIM ** -0.5)
    v = v.reshape(bsz, L, RET_HEADS, RET_HEAD_V)
    log_g = jnp.log(1.0 - jnp.exp2(-5.0 - jnp.arange(RET_HEADS, dtype=jnp.float32)))
    idx = jnp.arange(RET_CHUNK, dtype=jnp.float32)
    diff = idx[:, None] - idx[None, :]
    dmat = jnp.where(diff >= 0, jnp.exp(jnp.maximum(diff, 0.0)[None] * log_g[:, None, None]), 0.0)
    qc = q.reshape(bsz, nc, RET_CHUNK, RET_HEADS, RET_QK_DIM)
    kc = k.reshape(bsz, nc, RET_CHUNK, RET_HEADS, RET_QK_DIM)
    vc = v.reshape(bsz, nc, RET_CHUNK, RET_HEADS, RET_HEAD_V)
    inner = jnp.einsum('bnhij,bnjhe->bnihe', jnp.einsum('bnihd,bnjhd->bnhij', qc, kc) * dmat, vc)
    zeta = jnp.exp((RET_CHUNK - 1.0 - idx)[:, None] * log_g[None, :])
    chunk_kv = jnp.einsum('bnjhd,bnjhe->bnhde', kc * zeta[..., None], vc)
    chunk_decay = jnp.exp(RET_CHUNK * log_g)

    def step(r, s):
        return (r * chunk_decay[:, None, None] + s).astype(r.dtype), r

    r0 = jnp.zeros_like(chunk_kv[:, 0])
    _, prev = lax.scan(step, r0, jnp.moveaxis(chunk_kv, 1, 0))
    prev = jnp.moveaxis(prev, 0, 1)
    xi = jnp.exp((idx + 1.0)[:, None] * log_g[None, :])
    cross = jnp.einsum('bnihd,bnhde->bnihe', qc, prev) * xi[..., None]
    o = (inner + cross).reshape(bsz, L, RET_HEADS, RET_HEAD_V).astype(jnp.float32)
    mu = jnp.mean(o, axis=-1, keepdims=True)
    var = jnp.mean(jnp.square(o - mu), axis=-1, keepdims=True)
    o = ((o - mu) * lax.rsqrt(var + EPS)).reshape(bsz, L, RET_HEADS * RET_HEAD_V)
    o = (o * gn_g.astype(jnp.float32)).astype(g.dtype)
    return o * jax.nn.silu(g)

def t5_bucket(dist):
    is_small = dist < REL_MAX_EXACT
    d = jnp.maximum(dist, 1).astype(jnp.float32)
    large = REL_MAX_EXACT + (jnp.log(d / REL_MAX_EXACT) / math.log(REL_MAX_DIST / REL_MAX_EXACT)
                             * (REL_BUCKETS - REL_MAX_EXACT)).astype(jnp.int32)
    large = jnp.minimum(large, REL_BUCKETS - 1)
    return jnp.where(is_small, dist, large)

def swa_sink_attention(q, k, v, sinks, band_bias, band_mask):
    bsz, L, _ = q.shape
    nb = L // ATT_BLOCK
    q = q.reshape(bsz, nb, ATT_BLOCK, ATT_KV_HEADS, ATT_GROUP, ATT_HEAD_DIM)
    k = k.reshape(bsz, L, ATT_KV_HEADS, ATT_HEAD_DIM)
    v = v.reshape(bsz, L, ATT_KV_HEADS, ATT_HEAD_DIM)

    def band(t):
        tp = jnp.pad(t, ((0, 0), (ATT_BLOCK, 0), (0, 0), (0, 0)))
        tp = tp.reshape(bsz, nb + 1, ATT_BLOCK, ATT_KV_HEADS, ATT_HEAD_DIM)
        return jnp.concatenate([tp[:, :-1], tp[:, 1:]], axis=2)

    kb, vb = band(k), band(v)
    s = jnp.einsum('bnqkgd,bnskd->bnkgqs', q, kb).astype(jnp.float32) * (ATT_HEAD_DIM ** -0.5)
    s = jnp.where(band_mask[None, :, None, None], s + band_bias, NEG)
    sink = sinks.astype(jnp.float32).reshape(ATT_KV_HEADS, ATT_GROUP, 1, 1)
    m = jnp.maximum(jnp.max(s, axis=-1, keepdims=True), sink)
    e = jnp.exp(s - m)
    p = e / (jnp.sum(e, axis=-1, keepdims=True) + jnp.exp(sink - m))
    o = jnp.einsum('bnkgqs,bnskd->bnqkgd', p.astype(v.dtype), vb)
    return o.reshape(bsz, L, ATT_Q_HEADS * ATT_HEAD_DIM)

def second_inputs(seed: int = 0) -> dict:
    key = jax.random.key(seed)
    ks = iter(jax.random.split(key, 32))
    f32 = jnp.float32

    def nrm(shape, fan_in):
        return jax.random.normal(next(ks), shape, f32) * (fan_in ** -0.5)

    def gain(shape):
        return 1.0 + 0.1 * jax.random.normal(next(ks), shape, f32)

    x = jax.random.normal(next(ks), (BATCH, SEQ, D_MODEL), f32)
    ffn1_pre_g = gain((DEPTH, D_MODEL))
    ffn1_post_g = gain((DEPTH, D_MODEL))
    w_ffn1_in = nrm((DEPTH, D_MODEL, 2 * D_FF), D_MODEL)
    w_ffn1_out = nrm((DEPTH, D_FF, D_MODEL), D_FF)
    mix_pre_g = gain((DEPTH, D_MODEL))
    mix_post_g = gain((DEPTH, D_MODEL))
    w_in = nrm((DEPTH, D_MODEL, IN_WIDTH_2), D_MODEL)
    conv_w = nrm((DEPTH, SSD_CONV, SSD_CONV_DIM), SSD_CONV)
    conv_b = 0.1 * jax.random.normal(next(ks), (DEPTH, SSD_CONV_DIM), f32)
    dt0 = jnp.exp(jax.random.uniform(next(ks), (DEPTH, SSD_HEADS), f32,
                                     math.log(1e-3), math.log(1e-1)))
    dt_bias = dt0 + jnp.log(-jnp.expm1(-dt0))
    a_log = jnp.log(jax.random.uniform(next(ks), (DEPTH, SSD_HEADS), f32, 1.0, 16.0))
    d_skip = gain((DEPTH, SSD_HEADS))
    ssd_norm_g = gain((DEPTH, SSD_D_INNER))
    ret_gn_g = gain((DEPTH, RET_HEADS * RET_HEAD_V))
    attn_sinks = 0.5 * jax.random.normal(next(ks), (DEPTH, ATT_Q_HEADS), f32)
    rel_bias = 0.5 * jax.random.normal(next(ks), (REL_BUCKETS, ATT_Q_HEADS), f32)
    b_gate = 0.1 * jax.random.normal(next(ks), (DEPTH, N_BRANCH * D_MODEL), f32)
    w_branch = nrm((DEPTH, N_BRANCH, BRANCH_WIDTH, D_MODEL), BRANCH_WIDTH)
    w_out = nrm((DEPTH, D_MODEL, D_MODEL), D_MODEL)
    ffn2_pre_g = gain((DEPTH, D_MODEL))
    ffn2_post_g = gain((DEPTH, D_MODEL))
    w_ffn2_in = nrm((DEPTH, D_MODEL, 2 * D_FF), D_MODEL)
    w_ffn2_out = nrm((DEPTH, D_FF, D_MODEL), D_FF)
    return {"x": x, "ffn1_pre_g": ffn1_pre_g, "ffn1_post_g": ffn1_post_g,
            "w_ffn1_in": w_ffn1_in, "w_ffn1_out": w_ffn1_out,
            "mix_pre_g": mix_pre_g, "mix_post_g": mix_post_g, "w_in": w_in,
            "conv_w": conv_w, "conv_b": conv_b, "dt_bias": dt_bias, "a_log": a_log,
            "d_skip": d_skip, "ssd_norm_g": ssd_norm_g, "ret_gn_g": ret_gn_g,
            "attn_sinks": attn_sinks, "rel_bias": rel_bias, "b_gate": b_gate,
            "w_branch": w_branch, "w_out": w_out,
            "ffn2_pre_g": ffn2_pre_g, "ffn2_post_g": ffn2_post_g,
            "w_ffn2_in": w_ffn2_in, "w_ffn2_out": w_ffn2_out}

def second_block(x, ffn1_pre_g, ffn1_post_g, w_ffn1_in, w_ffn1_out, mix_pre_g, mix_post_g, w_in,
              conv_w, conv_b, dt_bias, a_log, d_skip, ssd_norm_g, ret_gn_g, attn_sinks, rel_bias,
              b_gate, w_branch, w_out, ffn2_pre_g, ffn2_post_g, w_ffn2_in, w_ffn2_out):
    bsz, L, _ = x.shape
    offsets = np.cumsum(IN_SPLIT_SIZES)[:-1].tolist()
    pos = jnp.arange(L, dtype=jnp.float32)
    inv = 1.0 / (ROPE_BASE ** (jnp.arange(0, RET_QK_DIM, 2, dtype=jnp.float32) / RET_QK_DIM))
    ang = pos[:, None] * inv[None, :]
    cos, sin = jnp.cos(ang), jnp.sin(ang)
    nb = L // ATT_BLOCK
    qi = jnp.arange(ATT_BLOCK)[:, None]
    sj = jnp.arange(2 * ATT_BLOCK)[None, :]
    dist = qi + ATT_BLOCK - sj
    blk = jnp.arange(nb)[:, None, None]
    band_mask = (dist >= 0) & (dist < WINDOW) & ((blk > 0) | (sj >= ATT_BLOCK))
    band_bias = jnp.transpose(rel_bias[t5_bucket(jnp.maximum(dist, 0))], (2, 0, 1))
    band_bias = band_bias.astype(jnp.float32).reshape(ATT_KV_HEADS, ATT_GROUP, ATT_BLOCK, 2 * ATT_BLOCK)

    for l in range(DEPTH):
        x = x + 0.5 * rmsnorm(swiglu_2(rmsnorm(x, ffn1_pre_g[l]), w_ffn1_in[l], w_ffn1_out[l]), ffn1_post_g[l])
        h = rmsnorm(x, mix_pre_g[l])
        (z, xbc, dt_raw, rq, rk, rv, rg, aq, ak, av, gate) = jnp.split(h @ w_in[l], offsets, axis=-1)
        y_ssd = ssd_mixer(z, xbc, dt_raw, conv_w[l], conv_b[l], dt_bias[l], a_log[l], d_skip[l], ssd_norm_g[l])
        y_ret = retention_mixer(rq, rk, rv, rg, ret_gn_g[l], cos, sin)
        y_att = swa_sink_attention(aq, ak, av, attn_sinks[l], band_bias, band_mask)
        ys = jnp.stack([y_ssd.astype(x.dtype), y_ret.astype(x.dtype), y_att.astype(x.dtype)], axis=2)
        branch = jnp.einsum('blmc,mcd->blmd', ys, w_branch[l])
        gates = jax.nn.sigmoid((gate + b_gate[l]).reshape(bsz, L, N_BRANCH, D_MODEL))
        y = jnp.sum(gates * branch, axis=2) @ w_out[l]
        x = x + rmsnorm(y, mix_post_g[l])
        x = x + 0.5 * rmsnorm(swiglu_2(rmsnorm(x, ffn2_pre_g[l]), w_ffn2_in[l], w_ffn2_out[l]), ffn2_post_g[l])
    return x


def setup_inputs(seed=0):
    out = dict(first_inputs(seed))
    for name, value in second_inputs(seed + 1).items():
        if name != "x":
            out[name + "_2"] = value
    return out


def reference(
    x, ffn1_norm, ffn1_w1, ffn1_w3, ffn1_w2, mix_norm, w_in, b_gate, attn_sink, pool_w,
    pool_scale, w_branch_attn, w_branch_pool, w_out, ffn2_norm, ffn2_w1, ffn2_w3, ffn2_w2,
    final_norm, ffn1_pre_g_2, ffn1_post_g_2, w_ffn1_in_2, w_ffn1_out_2, mix_pre_g_2,
    mix_post_g_2, w_in_2, conv_w_2, conv_b_2, dt_bias_2, a_log_2, d_skip_2, ssd_norm_g_2,
    ret_gn_g_2, attn_sinks_2, rel_bias_2, b_gate_2, w_branch_2, w_out_2, ffn2_pre_g_2,
    ffn2_post_g_2, w_ffn2_in_2, w_ffn2_out_2,
):
    x = first_block(
        x, ffn1_norm, ffn1_w1, ffn1_w3, ffn1_w2, mix_norm, w_in, b_gate, attn_sink, pool_w,
        pool_scale, w_branch_attn, w_branch_pool, w_out, ffn2_norm, ffn2_w1, ffn2_w3, ffn2_w2,
        final_norm,
    )
    return second_block(
        x, ffn1_pre_g_2, ffn1_post_g_2, w_ffn1_in_2, w_ffn1_out_2, mix_pre_g_2, mix_post_g_2,
        w_in_2, conv_w_2, conv_b_2, dt_bias_2, a_log_2, d_skip_2, ssd_norm_g_2, ret_gn_g_2,
        attn_sinks_2, rel_bias_2, b_gate_2, w_branch_2, w_out_2, ffn2_pre_g_2, ffn2_post_g_2,
        w_ffn2_in_2, w_ffn2_out_2,
    )


_drawn_inputs = setup_inputs


def setup_inputs(seed=0):
    import zlib

    import numpy as np

    out = dict(_drawn_inputs(seed))
    spreads = {}
    factors = {'b_gate': 5.766, 'attn_sink': 8.0, 'attn_sinks_2': 6.973}
    for name, (base, spread) in spreads.items():
        noise = np.random.default_rng([zlib.crc32(name.encode()), seed]).standard_normal(out[name].shape)
        drawn = base * np.exp(spread * noise) if base else spread * noise
        out[name] = __import__('jax').numpy.asarray(drawn.astype(out[name].dtype))
    for name, factor in factors.items():
        out[name] = (out[name] * factor).astype(out[name].dtype)
    return out
```

```python
from contextlib import ExitStack

import numpy as np

import concourse.bass as bass
from concourse import mybir

ALU = mybir.AluOpType
ACT = mybir.ActivationFunctionType
AX = mybir.AxisListType
F32 = mybir.dt.float32
F32R = mybir.dt.float32r
ds = bass.ds

P = 128
EPS = 1e-6
SLOTS = 3
UNIT = 2048
NARROW = 256


class Table:

    def __init__(self, n, uses):
        self.n, self.at, self.total, k = n, {}, [0] * n, 0
        for name, count in uses:
            for i in range(count):
                self.total[k % n] += 1
                self.at[name, i] = (k % n, self.total[k % n])
                k += 1

    def use(self, name, i=0):
        return self.at[name, i]


def tables(block, steps):
    if block == 0:
        mix_units = 21
        mix_work = [("turn_m", 4), ("pool", 2), ("qkT", 4), ("scores0", 8), ("probsT0", 8), ("mixp", 2), ("turn_o", 2),
                    ("turn_y", 4)]
        splits = [("turn_m", 4), ("mixp", 2), ("turn_o", 2), ("turn_y", 4)]
        chunks = [("q", 1), ("kv", 1), ("p", 1), ("gate", 3), ("pv0", 1), ("gate_b", 1), ("br_a", 2), ("br_p", 2)]
        norms = ["f1", "m", "f2"]
    else:
        mix_units = 57
        mix_work = [("turn_m", 4), ("rqkT", 4), ("decay", 4), ("ret", 4), ("turn_r", 4), ("qkT", 6),
                    ("scores0", 8), ("probsT0", 8), ("scores1", 8), ("probsT1", 8), ("turn_o", 4),
                    ("xbcT", 6), ("xsT", 4), ("cb", 2), ("acs", 1), ("seg", 16), ("turn_s", 4), ("turn_y", 4)]
        splits = [("turn_m", 4), ("turn_r", 4), ("turn_o", 4), ("turn_s", 4), ("turn_y", 4)]
        chunks = [("rqk", 2), ("rv", 2), ("gate_r", 2), ("rg", 2), ("aq", 2), ("akv", 1), ("br_r", 2),
                  ("gate_a0", 1), ("pv0", 1), ("gate_a1", 1), ("pv1", 1), ("br_a", 2),
                  ("xbc", 3), ("dt", 1), ("z", 2), ("gate_s", 2), ("ys", 2), ("br_s", 2)]
        norms = ["f1", "p1", "m", "s", "pm", "f2", "p2"]
    return dict(
        units=Table(SLOTS, [("all", 6 * steps + mix_units)]),
        work=Table(4, [("turn_f1", 4)] + mix_work + [("turn_f2", 4)]),
        split=Table(1, [("turn_f1", 4)] + splits + [("turn_f2", 4)]),
        chunks=Table(2, chunks),
        norms=Table(1, [(n, 1) for n in norms]),
    )


def build(nc, a):
    depth, dm, d_ff = a["ffn1_w1"].shape
    kd = dm // P
    half = dm // 2
    steps = d_ff // NARROW
    assert d_ff % NARROW == 0 and dm == 1024 and steps >= 2

    T = [tables(b, steps) for b in range(2)]
    w_f = {
        (0, "f1"): ("ffn1_w1", "ffn1_w3", 0, "ffn1_w2"),
        (0, "f2"): ("ffn2_w1", "ffn2_w3", 0, "ffn2_w2"),
        (1, "f1"): ("w_ffn1_in_2", "w_ffn1_in_2", d_ff, "w_ffn1_out_2"),
        (1, "f2"): ("w_ffn2_in_2", "w_ffn2_in_2", d_ff, "w_ffn2_out_2"),
    }

    with ExitStack() as ctx:
        def sb(name, shape, dt=F32):
            return ctx.enter_context(nc.sbuf_tensor(name, shape, dt))

        def sem(name):
            return ctx.enter_context(nc.semaphore(name))

        raw = sb("raw", [P, SLOTS, UNIT])
        w_hi = sb("w_hi", [P, SLOTS, UNIT], F32R)
        w_lo = sb("w_lo", [P, SLOTS, UNIT], F32R)
        h = sb("h", [P, 2, dm])
        xt_hi = sb("xt_hi", [P, kd, 2 * P], F32R)
        xt_lo = sb("xt_lo", [P, kd, 2 * P], F32R)
        yt_hi = sb("yt_hi", [P, kd, 2 * P], F32R)
        yt_lo = sb("yt_lo", [P, kd, 2 * P], F32R)
        ident = sb("ident", [P, P])
        field = sb("field", [P, 14400])
        vec = sb("vec", [P, 100])
        row = sb("row", [P, 64])
        bias = sb("bias", [P, 2, dm])
        causal = sb("causal", [P, 2 * P])
        rope1 = sb("rope1", [P, 2, 2, 16])
        blk = sb("blk", [P, 5632])
        sm = sb("sm", [P, 768])
        post = sb("post", [P, dm])
        sq = sb("sq", [P, 8])
        ms = sb("ms", [P, 2])
        rs = sb("rs", [P, 2])
        rp = sb("rp", [P, 2])
        minus_half = sb("minus_half", [P, 8])

        hid = field[:, 0:2 * NARROW].rearrange("p (r n) -> p r n", r=2)
        act_gate = field[:, 2 * NARROW:4 * NARROW].rearrange("p (r n) -> p r n", r=2)
        junk = field[:, 1024:2048].bitcast(mybir.dt.bfloat16)
        tmp = field[:, 2048:4096].rearrange("p (i n) -> p i n", i=4)

        band = blk[:, 0:512].rearrange("p (r k) -> p r k", r=2)
        window = blk[:, 512:2560].rearrange("p (g t s) -> p g t s", g=4, t=2)
        pool_w = blk[:, 2560:3072].rearrange("p (g d) -> p g d", g=4)
        decay = blk[:, 0:1024].rearrange("p (h q) -> p h q", h=4)
        rope2 = blk[:, 1024:1536].rearrange("p (r s n) -> p r s n", r=2, s=2)
        rel_bias = blk[:, 1536:5632].rearrange("p (h k) -> p h k", h=16)

        work = [ctx.enter_context(nc.psum_tensor(f"work{i}", [P, 512], F32)) for i in range(4)]
        acc = [ctx.enter_context(nc.psum_tensor(f"acc{i}", [P, 512], F32)) for i in range(4)]

        def view(at, *shape):
            n = int(np.prod(shape))
            assert at + n <= 14400
            names = "abcd"[:len(shape)]
            return field[:, at:at + n].rearrange(f"p ({' '.join(names)}) -> p {' '.join(names)}",
                                                 **dict(zip(names, shape)))

        A = dict(
            gate=[view(0, 2, dm), view(2048, 2, dm)],
            qk=view(4096, 2, 640), v=view(5888, 2, P),
            kk=view(9856, 2, 2, 2, P),
            p=view(6144, 2, 512), o=view(6144, 2, 512),
            qT=view(7168, 8, 2 * P), e=lambda i: view(9216 + 512 * i, 2, 2 * P), pT=view(4096, 2, 512), pooled=view(13312, 4, 2 * P),
            rope=view(9216, 2, 2, 160),
        )
        mixed2 = view(0, 2, dm)
        R = dict(qk=view(2048, 2, dm), v=view(4096, 2, dm), g=view(6144, 2, dm), qT=view(8192, 8, 2 * P),
                 w=view(10240, 4, 3 * P), rope=(view(8192, 8, P), view(9216, 8, P)))
        B = dict(q=view(11776, 2, dm), o=view(11776, 2, dm), k=view(2048, 2, P), v=view(2304, 2, P),
                 kk=view(2560, 2, 2, 2, P), pT=view(2560, 2, 512), qT=view(3584, 12, 2 * P), gate=view(9728, 2, dm),
                 e=lambda i: view(6656 + 256 * i, 2, P) if i < 4 else view(7680 + 512 * (i - 4), 2, 2 * P))
        S = dict(rows=view(2048, 2, 1536), padded=view(5120, 12, 2 * P + 3), conv=view(8228, 12, 2 * P),
                 z=view(11300, 2, dm), cb=view(13348, 2, 3 * P), skip=view(2048, 2, dm), xdt=view(4096, 2, dm),
                 gate=view(6144, 2, dm), seg=view(8228, 8, 3 * P), y=view(2048, 2, dm))
        heads16 = lambda at: sm[:, at:at + 32].rearrange("p (r h) -> p r h", r=2)
        dt_x, dt_e, dt_z, dt_z2, dt_q, dt, da, a_cs = (heads16(96 + 32 * i) for i in range(8))
        dt_abs = heads16(480)
        a_exp = sm[:, 352:368]
        bn = sm[:, 384:432].rearrange("p (i n) -> p i n", i=8)
        mv = sm[:, 432:448].rearrange("p (i n) -> p i n", i=8)
        ret_var, ret_rstd = sm[:, 448:456], sm[:, 456:464]

        top = sm[:, 0:16].rearrange("p (r h) -> p r h", r=2)
        minus_top = sm[:, 16:32].rearrange("p (r h) -> p r h", r=2)
        total = sm[:, 32:48].rearrange("p (r h) -> p r h", r=2)
        sink_e = sm[:, 48:64].rearrange("p (r h) -> p r h", r=2)
        inv = sm[:, 64:80].rearrange("p (r h) -> p r h", r=2)

        raw_loaded = [sem(f"raw_loaded{s}") for s in range(SLOTS)]
        hi_split = [sem(f"hi_split{s}") for s in range(SLOTS)]
        unit_split = [sem(f"unit_split{s}") for s in range(SLOTS)]
        unit_used = [sem(f"unit_used{s}") for s in range(SLOTS)]
        work_filled = [sem(f"work_filled{i}") for i in range(4)]
        work_read = [sem(f"work_read{i}") for i in range(4)]
        hi_turned = sem("hi_turned")
        consts_loaded = sem("consts_loaded")
        x_loaded = sem("x_loaded")
        vec_loaded = sem("vec_loaded")
        gain1_loaded = sem("gain1_loaded")
        post_loaded = sem("post_loaded")
        blk_loaded = sem("blk_loaded")
        bias_loaded = [sem(f"bias_loaded{i}") for i in range(2)]
        chunk_read = [sem(f"chunk_read{i}") for i in range(2)]
        dve_step = sem("dve_step")
        rows_ready = sem("rows_ready")
        tops_ready = sem("tops_ready")
        probs_ready = sem("probs_ready")
        pv_done = sem("pv_done")
        gate_ready = sem("gate_ready")
        mixed_ready = sem("mixed_ready")
        table_ready = sem("table_ready")
        scratch_stored = sem("scratch_stored")
        ret_var_ready = sem("ret_var_ready")
        ret_rstd_ready = sem("ret_rstd_ready")
        ret_ready = sem("ret_ready")
        dt_abs_ready = sem("dt_abs_ready")
        dt_exp_ready = sem("dt_exp_ready")
        da_ready = sem("da_ready")
        padded_ready = sem("padded_ready")
        conv_ready = sem("conv_ready")
        xc_ready = sem("xc_ready")
        seg_exp = sem("seg_exp")
        seg_ready = sem("seg_ready")
        y_done = sem("y_done")
        y_ready = sem("y_ready")
        h_ready = sem("h_ready")
        squared = sem("squared")
        mean_ready = sem("mean_ready")
        rs_ready = sem("rs_ready")
        silu_ready = sem("silu_ready")
        hidden_ready = sem("hidden_ready")
        hidden_turned = sem("hidden_turned")
        hidden_hi = sem("hidden_hi")
        hidden_split = sem("hidden_split")
        pair_added = sem("pair_added")
        post_scaled = sem("post_scaled")
        exponent_set = sem("exponent_set")
        stored = sem("stored")

        def count(kind, block, l, name, i=0):
            slot, k = T[block][kind].use(name, i)
            before = sum(T[b][kind].total[slot] for b in range(block)) * depth
            return slot, l * T[block][kind].total[slot] + (before + k)

        def unit_count(block, l, pos):
            slot, per, first = pos % SLOTS, T[block]["units"].total, T[0]["units"].total
            return slot, l * per[slot] + ((first[slot] * depth if block else 0) + pos // SLOTS + 1)

        def used_count(block, l, pos, r=1, j=0):
            slot, n = unit_count(block, l, pos)
            return slot, (n + j) * 2 + (r + 1)

        STAGES = 3

        def h_count(block, l, stage):
            return l * (4 * STAGES) + (4 + (4 * STAGES * depth + 4 if block else 0) + 4 * stage)

        def stage_of(block, name):
            return {"f1": 0, "m": 1, "f2": 2}[name]

        def norm_count(block, l, name):
            return count("norms", block, l, name)[1] + (1 if block else 0)

        def ffn_count(block, l, name, per):
            return l * (2 * per) + per * ((2 * depth if block else 0) + (name == "f2"))

        first_unit = {(b, "f1"): 0 for b in range(2)}
        for b in range(2):
            n = sum(T[b]["units"].total)
            first_unit[b, "m"] = 3 * steps
            first_unit[b, "f2"] = n - 3 * steps
            assert n % SLOTS == 0 and first_unit[b, "f2"] % SLOTS == 0

        def chunk_count(block, l, name, i=0, r=1):
            pair, n = count("chunks", block, l, name, i)
            return pair, n * 2 + (r + 1)

        def events(block, l, per, k):
            return l * per[block] + ((per[0] * depth if block else 0) + k)

        PASSES, ROWS, GATES = (1, 2), (1, 2), (8, 12)

        def key_tiles(block, r):
            return 2 if not block or r else 1

        def gain(name):
            return {"f1": 0, "m": 8, "f2": 16, "s": 24, "ret": 32}[name]

        block_ = ctx.enter_context(nc.Block())

        @block_.sync
        def _(sp):
            def load(block, l, pos, parts, j=0):
                slot, n = unit_count(block, l, pos)
                n = n + j
                sp.wait_ge(unit_split[slot], n)
                for dst, src in parts(raw[:, slot, :]):
                    sp.dma_start(dst, src).then_inc(raw_loaded[slot], 16)

            def rows(name, l, k0, n, c0, cols):
                w = a[name].rearrange("l (t p) n -> l p t n", p=P)
                return w[ds(l, 1), :, k0:k0 + n, ds(c0, cols) if not isinstance(c0, int) else slice(c0, c0 + cols)] \
                    .rearrange("l p t n -> (l p) t n")

            def gate_up(block, name, l, j, k0):
                wg, wu, off, _ = w_f[block, name]

                def parts(dst):
                    d = dst.rearrange("p (t s n) -> p t s n", t=4, s=2)
                    return ((d[:, :, 0, :], rows(wg, l, k0, 4, j * NARROW, NARROW)),
                            (d[:, :, 1, :], rows(wu, l, k0, 4, j * NARROW + off, NARROW)))
                return parts

            def down(block, name, l, j):
                wd = a[w_f[block, name][3]].rearrange("l (t p) n -> l t p n", p=P)

                def parts(dst):
                    d = dst.rearrange("p (t n) -> p t n", t=2)
                    return tuple((d[:, t, :], wd[ds(l, 1), ds(j * 2 + t, 1) if not isinstance(j, int)
                                                 else slice(j * 2 + t, j * 2 + t + 1), :, :]
                                  .rearrange("l t p n -> (l t p) n")) for t in range(2))
                return parts

            def small(block, l, name):
                if block or name == "f1":
                    sp.wait_ge(h_ready, h_count(block, l, stage_of(block, name)))
                if name == "f2":
                    sp.dma_start(vec[:, 0:8], a["gain1"][ds(l + (depth * block + 1), 1), :, :]
                                 .rearrange("l p n -> (l p) n")).then_inc(gain1_loaded, 16)
                if block:
                    src = {"f1": "ffn1_post_g_2", "f2": "ffn2_post_g_2", "m": "mix_post_g_2"}[name]
                    sp.dma_start(post[:, :], a[src][ds(l, 1), :].partition_broadcast(P)).then_inc(post_loaded, 16)
                if name != "f1":
                    return
                v = a[f"vec{block}"]
                sp.dma_start(vec[:, 8:8 + v.shape[2]], v[ds(l, 1), :, :].rearrange("l p n -> (l p) n")) \
                    .then_inc(vec_loaded, 16)
                w = a[f"row{block}"]
                sp.dma_start(row[:, 0:w.shape[1]], w[ds(l, 1), :].partition_broadcast(P)).then_inc(vec_loaded, 16)

            def mixer_small(block, l):
                if not block:
                    for dst, src in ((band, "band"), (window, "window")):
                        sp.dma_start(dst, a[src]).then_inc(blk_loaded, 16)
                    sp.dma_start(pool_w, a["pool_w"][ds(l, 1), :, :, :].rearrange("l g c d -> (l c) g d")) \
                        .then_inc(blk_loaded, 16)
                b = a["b_gate_2" if block else "b_gate"]
                for i in range(2):
                    sp.dma_start(bias[:, i, :], b[ds(l, 1), (i + block) * dm:(i + block + 1) * dm].partition_broadcast(P)) \
                        .then_inc(bias_loaded[i], 16)

            def ffn(block, name, l):
                u = first_unit[block, name]
                load(block, l, u, gate_up(block, name, l, 0, 0))
                load(block, l, u + 1, gate_up(block, name, l, 0, 4))
                small(block, l, name)
                with sp.Fori(0, steps - 1) as j:
                    load(block, l, u + 2, gate_up(block, name, l, j + 1, 0), j)
                    load(block, l, u + 3, gate_up(block, name, l, j + 1, 4), j)
                    load(block, l, u + 4, down(block, name, l, j), j)
                if name == "f1":
                    mixer_small(block, l)
                load(block, l, u + 3 * steps - 1, down(block, name, l, steps - 1))

            def whole(name, l, k0, c0, cols=512, kts=4):
                def parts(dst):
                    d = dst[:, 0:kts * cols].rearrange("p (t n) -> p t n", t=kts)
                    n = kts // 2
                    return tuple((d[:, i * n:(i + 1) * n, :], rows(name, l, k0 + i * n, n, c0, cols)) for i in (1, 0))
                return parts

            def mixer1(l):
                m = first_unit[0, "m"]
                at = iter(range(m, m + 21))
                for n, c0 in enumerate((0, 512, 768, 1280, 1792, 2304, 2816)):
                    if c0 == 512:
                        load(0, l, next(at), whole("w_in", l, 0, 512, 256, 8))
                        continue
                    for k0 in (0, 4):
                        load(0, l, next(at), whole("w_in", l, k0, c0))
                for name in ("w_branch_attn", "w_branch_pool"):
                    for c0 in (0, 512):
                        load(0, l, next(at), whole(name, l, 0, c0))
                for c0 in (0, 512):
                    for k0 in (0, 4):
                        load(0, l, next(at), whole("w_out", l, k0, c0))

            def mixer2(l):
                m = first_unit[1, "m"]
                at = iter(range(m, m + 57))

                def chunks(name, c0, n, k0=0, col=lambda c: c):
                    for c in range(n):
                        for k in (0, 4):
                            load(1, l, next(at), whole(name, l, k0 + k, c0 + 512 * c))

                def branch(i, between=lambda: None):
                    w = a["w_branch_2"].rearrange("l m (t p) n -> l m p t n", p=P)
                    for c in range(2):
                        for k in (0, 4):
                            def parts(dst, c=c, k=k):
                                d = dst.rearrange("p (t n) -> p t n", t=4)
                                return tuple((d[:, j:j + 2, :], w[ds(l, 1), i, :, k + j:k + j + 2, c * 512:(c + 1) * 512]
                                              .rearrange("l p t n -> (l p) t n")) for j in (2, 0))
                            load(1, l, next(at), parts)
                            between()
                            between = lambda: None

                chunks("w_in_2", 2576, 1)
                small(1, l, "m")
                chunks("w_in_2", 3088, 3)
                chunks("w_in_2", 6928 + dm, 2)
                chunks("w_in_2", 4624, 2)
                chunks("w_in_2", 5648, 2)
                for k in (0, 4):
                    load(1, l, next(at), whole("w_in_2", l, k, 6672, 256))
                pair, n = chunk_count(1, l, "gate_r", 1)
                sp.wait_ge(chunk_read[pair], n)
                branch(1, lambda: sp.dma_start(bias[:, 0, :], a["b_gate_2"][ds(l, 1), 0:dm].partition_broadcast(P))
                       .then_inc(bias_loaded[0], 16))
                chunks("w_in_2", 6928 + 2 * dm, 2)
                branch(2)
                chunks("w_in_2", 1024, 3)
                load(1, l, next(at), whole("w_in_2", l, 0, 2560, 16, 8))
                chunks("w_in_2", 0, 2)
                chunks("w_in_2", 6928, 2)
                branch(0)
                chunks("w_out_2", 0, 2)

            sp.dma_start(field[:, 0:2 * dm].rearrange("p (r n) -> p r n", r=2),
                         a["x"].rearrange("b (r p) n -> p (b r) n", p=P)).then_inc(x_loaded, 16)
            sp.dma_start(vec[:, 0:8], a["gain1"][0]).then_inc(gain1_loaded, 16)
            sp.dma_start(field[0:32, 4096:4112], a["rel_bias_2"]).then_inc(consts_loaded, 16)
            sp.dma_start(field[0:32, 4200:4584], a["one_hot"]).then_inc(consts_loaded, 16)
            sp.dma_start(field[0:16, 4600:4984], a["unseen"]).then_inc(consts_loaded, 16)
            sp.dma_start(ident[:, :], a["ident"]).then_inc(consts_loaded, 16)
            sp.dma_start(causal[:, :], a["causal"]).then_inc(consts_loaded, 16)
            sp.dma_start(rope1[:, :, :, :], a["rope1"]).then_inc(consts_loaded, 16)
            for block in range(2):
                with sp.Fori(0, depth) as l:
                    ffn(block, "f1", l)
                    (mixer2 if block else mixer1)(l)
                    ffn(block, "f2", l)
                if not block:
                    sp.dma_start(post[:, :], a["final_norm"].rearrange("(a n) -> a n", a=1).partition_broadcast(P)) \
                        .then_inc(post_loaded, 16)
                    sp.wait_ge(h_ready, 4 + 4 * (STAGES * depth - 1))
                    for dst, src in ((decay, a["decay"]), (rope2, a["rope2"])):
                        sp.dma_start(dst, src).then_inc(blk_loaded, 16)
                    sp.wait_ge(scratch_stored, 16)
                    sp.dma_start(rel_bias, bass.AP(a["scratch"].tensor, P - 1,
                                                   [[3 * P - 1, P], [3 * P * P, 16], [1, 2 * P]])) \
                        .then_inc(blk_loaded, 16)
            for pos in range(2):
                load(1, depth, pos, gate_up(1, "f1", 0, 0, 4 * pos))
            sp.wait_ge(h_ready, 8 * STAGES * depth + 8)
            sp.dma_start(a["out"].rearrange("b (r p) n -> p (b r) n", p=P), h[:, :, :]).then_inc(stored, 16)
            sp.wait_ge(stored, 16)

        @block_.gpsimd
        def _(pool):
            nc.gpsimd.memset(minus_half[:, :], -0.5).then_inc(exponent_set, 1)
            pool.wait_ge(exponent_set, 1)

            def power(dst, n):
                pool.wait_ge(mean_ready, n)
                nc.gpsimd.tensor_tensor(dst[:, :], ms[:, :], minus_half[:, 0:2], ALU.pow).then_inc(rs_ready, 1)

            for block in range(2):
                with pool.Fori(0, depth) as l:
                    for name in ("f1", "m", "f2"):
                        if block and name == "m":
                            power(rs, norm_count(block, l, "m"))
                            pool.wait_ge(ret_var_ready, l + 1)
                            nc.gpsimd.tensor_tensor(ret_rstd, ret_var, minus_half[:, :], ALU.pow) \
                                .then_inc(ret_rstd_ready, 1)
                            power(rp, norm_count(block, l, "s"))
                            power(rp, norm_count(block, l, "pm"))
                            continue
                        power(rs, norm_count(block, l, name))
                        if block:
                            power(rp, norm_count(block, l, "p" + name[1]))
                if not block:
                    power(rs, sum(T[0]["norms"].total) * depth + 1)


        @block_.tensor
        def _(pe):
            for s in range(SLOTS):
                pe.sem_inc(unit_used[s], 2)
            pe.wait_ge(consts_loaded, 96)
            nc.tensor.matmul(acc[0][0:16, 0:3 * P], field[0:32, 4096:4112], field[0:32, 4200:4584], start=True,
                             stop=True).then_inc(table_ready, 1)

            def product(x_hi, x_lo, kt, r, slot, w0, cols, out, start, stop):
                k, w = slice(r * P, (r + 1) * P), slice(w0, w0 + cols)
                for n, (x, y) in enumerate(((x_hi, w_hi), (x_hi, w_lo), (x_lo, w_hi))):
                    last = nc.tensor.matmul(out, x[:, kt, k], y[:, slot, w], start=start and n == 0,
                                            stop=stop and n == 2)
                return last

            def transposes(bank, src, c):
                for t in range(2):
                    for r in range(2):
                        last = nc.tensor.transpose(work[bank][:, (2 * t + r) * P:(2 * t + r + 1) * P],
                                                   src[:, r, c + t * P:c + (t + 1) * P], ident[:, :])
                return last

            def turn(block, l, name, src, kts, wait):
                for i in range(kts // 2):
                    bank, n = count("work", block, l, name, i)
                    wait(i)
                    pe.wait_ge(work_read[bank], n)
                    transposes(bank, src, 2 * i * P).then_inc(work_filled[bank], 1)

            def turned(block, l, name, i):
                bank, n = count("work", block, l, name, i)
                pe.wait_ge(work_read[bank], n + 1)

            def turn_h(block, l, name):
                first = 2 if block or name == "f2" else 1
                turn(block, l, "turn_" + name, h, kd, lambda i: pe.wait_ge(
                    h_ready, h_count(block, l, stage_of(block, name)) - (first if i < kd // 4 else 0)))

            def ffn(block, name, l):
                u = first_unit[block, name]
                hidden_before = ffn_count(block, l, name, 2 * steps)
                steps_before = ffn_count(block, l, name, steps)

                def gate_up(pos, j, first=False):
                    for q in range(2):
                        slot, n = unit_count(block, l, pos + q)
                        pe.wait_ge(unit_split[slot], n + j + 1)
                        for r in range(2):
                            if q == 0 and not first:
                                pe.wait_ge(hidden_ready, hidden_before + (j * 2 + (r + 1)))
                            for t in range(4):
                                kt = 4 * q + t
                                if first and r == 0 and kt % 2 == 0:
                                    turned(block, l, "turn_" + name, kt // 2)
                                if first and kt == 0 and r == 0:
                                    turned(block, l, "turn_" + name, 2)
                                    turned(block, l, "turn_" + name, 3)
                                last = product(xt_hi, xt_lo, kt, r, slot, t * 512, 512, work[2 + r][:, :],
                                               kt == 0, kt == kd - 1)
                            last.then_inc(unit_used[slot], 1)

                def turn_hidden(j):
                    pe.wait_ge(hidden_ready, hidden_before + (j * 2 + 2))
                    transposes(0, hid, 0).then_inc(hidden_turned, 1)

                def down(pos, j, step, first=False, end=False):
                    slot, n = unit_count(block, l, pos)
                    pe.wait_ge(unit_split[slot], n + j + 1)
                    pe.wait_ge(hidden_split, steps_before + (step + 1))
                    for r in range(2):
                        for c in range(2):
                            for t in range(2):
                                last = product(yt_hi, yt_lo, t, r, slot, t * dm + c * half, half,
                                               acc[2 * r + c][:, :], first and t == 0, end and t == 1)
                        last.then_inc(unit_used[slot], 1)

                turn_h(block, l, name)
                gate_up(u, 0, True)
                turn_hidden(0)
                gate_up(u + 2, 0)
                down(u + 4, 0, 0, True)
                turn_hidden(1)
                with pe.Fori(1, steps - 1) as j:
                    gate_up(u + 2, j)
                    down(u + 4, j, j)
                    turn_hidden(j + 1)
                down(u + 3 * steps - 1, 0, steps - 1, False, True)

            def project(block, l, name, i, units, x, kts=4, cols=512, turn_name=None):
                pair, n = count("chunks", block, l, name, i)
                pe.wait_ge(chunk_read[pair], n * 2)
                for q, pos in enumerate(units):
                    slot, nu = unit_count(block, l, pos)
                    pe.wait_ge(unit_split[slot], nu + 1)
                    for r in range(2):
                        for t in range(kts):
                            kt = kts * q + t
                            if turn_name and r == 0 and kt % 2 == 0:
                                turned(block, l, turn_name, kt // 2)
                            last = product(x[0], x[1], kt, r, slot, t * cols, cols, acc[2 * pair + r][:, 0:cols],
                                           kt == 0, q == len(units) - 1 and t == kts - 1)
                        last.then_inc(unit_used[slot], 1)

            def project_out(block, l, c, units, turn_name=None):
                for q, pos in enumerate(units):
                    slot, nu = unit_count(block, l, pos)
                    pe.wait_ge(unit_split[slot], nu + 1)
                    for r in range(2):
                        for t in range(4):
                            kt = 4 * q + t
                            if turn_name and r == 0 and kt % 2 == 0:
                                turned(block, l, turn_name, kt // 2)
                            last = product(yt_hi, yt_lo, kt, r, slot, t * 512, 512, acc[2 * r + c][:, :],
                                           kt == 0, kt == kd - 1)
                        last.then_inc(unit_used[slot], 1)

            def fill(block, l, name, i=0):
                bank, n = count("work", block, l, name, i)
                pe.wait_ge(work_read[bank], n)
                return work[bank], work_filled[bank]

            def scores(block, l, g, qT, q_block, k_block):
                for r in range(2):
                    cols = P * key_tiles(block, r)
                    for hp in range(4):
                        bank, filled = fill(block, l, f"scores{g}", 4 * r + hp)
                        for s in range(2):
                            last = nc.tensor.matmul(bank[:, s * 256:s * 256 + cols],
                                                    qT[:, q_block(hp), r * P:(r + 1) * P],
                                                    qT[:, k_block(hp) + s, 0:cols], start=True, stop=True)
                        last.then_inc(filled, 1)

            def probs_by_v(block, l, g, i, e, pT, v, kv):
                r, hp = divmod(i, 4)
                pair, n = count("chunks", block, l, f"pv{g}")
                if i == 0:
                    pe.wait_ge(chunk_read[pair], n * 2)
                turned(block, l, f"probsT{g}", i)
                nk = key_tiles(block, r)
                for s in range(2):
                    c = (2 * hp + s) * 64
                    for kt in range(nk):
                        last = nc.tensor.matmul(acc[2 * pair + r][:, c:c + 64],
                                                pT[:, i % 2, (s * nk + kt) * P:(s * nk + kt + 1) * P],
                                                v[:, kt, kv(hp) * 64:kv(hp) * 64 + 64], start=kt == 0, stop=kt == nk - 1)
                last.then_inc(pv_done, 1)

            def probs(block, l, g, r, e, pT, v, kv):
                nk = key_tiles(block, r)
                for i in range(4 * r, 4 * r + 4):
                    bank, filled = fill(block, l, f"probsT{g}", i)
                    pe.wait_ge(probs_ready, events(block, l, [8 * n for n in PASSES], 8 * g + i + 1))
                    for s in range(2):
                        for kt in range(nk):
                            last = nc.tensor.transpose(bank[:, (s * nk + kt) * P:(s * nk + kt + 1) * P],
                                                       e(i)[:, s, kt * P:(kt + 1) * P], ident[:, :])
                    last.then_inc(filled, 1)
                    if i > 4 * r:
                        probs_by_v(block, l, g, i - 1, e, pT, v, kv)
                probs_by_v(block, l, g, 4 * r + 3, e, pT, v, kv)

            def turn_mixed(block, l, src):
                turn(block, l, "turn_y", src, kd, lambda i: pe.wait_ge(
                    mixed_ready, events(block, l, (4, 4), 2 * (i // 2) + 2)))

            def mixer1(l):
                m = first_unit[0, "m"]
                xt, yt = (xt_hi, xt_lo), (yt_hi, yt_lo)
                turn_h(0, l, "m")
                project(0, l, "q", 0, (m, m + 1), xt, turn_name="turn_m")
                project(0, l, "kv", 0, (m + 2,), xt, 8, 256)
                project(0, l, "p", 0, (m + 3, m + 4), xt)
                project(0, l, "gate", 0, (m + 5, m + 6), xt)
                pe.wait_ge(blk_loaded, events(0, l, (48, 48), 48))
                pair, n = chunk_count(0, l, "p")
                pe.wait_ge(chunk_read[pair], n)
                for i in range(2):
                    bank, filled = fill(0, l, "pool", i)
                    for s in range(2):
                        for t in range(2):
                            last = nc.tensor.matmul(bank[:, s * 256:(s + 1) * 256],
                                                    A["p"][:, t, (2 * i + s) * P:(2 * i + s + 1) * P],
                                                    window[:, 2 * i + s, t, :], start=t == 0, stop=t == 1)
                    last.then_inc(filled, 1)
                pe.wait_ge(rows_ready, events(0, l, ROWS, 1))
                for i in range(4):
                    bank, n = count("work", 0, l, "qkT", i)
                    pe.wait_ge(work_read[bank], n)
                    src, c = (A["qk"], 2 * i * P) if i < 2 else \
                        (A["kk"].rearrange("p r g s n -> p r (g s n)"), 2 * (i - 2) * P)
                    transposes(bank, src, c).then_inc(work_filled[bank], 1)
                project(0, l, "gate", 1, (m + 7, m + 8), xt)
                for i in range(4):
                    turned(0, l, "qkT", i)
                scores(0, l, 0, A["qT"], lambda hp: hp, lambda hp: 4 + 2 * (hp // 2))
                project(0, l, "gate", 2, (m + 9, m + 10), xt)
                probs(0, l, 0, 0, A["e"], A["pT"], A["v"], lambda hp: hp // 2)
                project(0, l, "gate_b", 0, (m + 11, m + 12), xt)
                probs(0, l, 0, 1, A["e"], A["pT"], A["v"], lambda hp: hp // 2)
                for i in range(2):
                    bank, filled = fill(0, l, "mixp", i)
                    turned(0, l, "pool", i)
                    for s in range(2):
                        last = nc.tensor.matmul(bank[:, s * 256:(s + 1) * 256], pool_w[:, 2 * i + s, :],
                                                A["pooled"][:, 2 * i + s, :], start=True, stop=True)
                    last.then_inc(filled, 1)
                pair, n = chunk_count(0, l, "pv0")
                turn(0, l, "turn_o", A["o"], 4, lambda i: pe.wait_ge(chunk_read[pair], n))
                for c in range(2):
                    project(0, l, "br_a", c, (m + 13 + c,), yt, turn_name="turn_o" if c == 0 else None)
                turned(0, l, "mixp", 0)
                turned(0, l, "mixp", 1)
                upper = (yt_hi[:, 4:8, :], yt_lo[:, 4:8, :])
                for c in range(2):
                    project(0, l, "br_p", c, (m + 15 + c,), upper)
                turn_mixed(0, l, A["gate"][0])
                for c in range(2):
                    project_out(0, l, c, (m + 17 + 2 * c, m + 18 + 2 * c), "turn_y" if c == 0 else None)

            def mixer2(l):
                m = first_unit[1, "m"]
                xt, yt = (xt_hi, xt_lo), (yt_hi, yt_lo)

                def chunk(name, c, first, x=xt, turn_name=None, **kw):
                    project(1, l, name, c, (m + first, m + first + 1), x, turn_name=turn_name, **kw)

                def transposed(name, src, tiles, k0=0):
                    for i in range(tiles // 2):
                        bank, n = count("work", 1, l, name, k0 + i)
                        pe.wait_ge(work_read[bank], n)
                        transposes(bank, src, 2 * i * P).then_inc(work_filled[bank], 1)

                turn_h(1, l, "m")
                chunk("rqk", 0, 0, turn_name="turn_m")
                chunk("rqk", 1, 2)
                for c in range(2):
                    chunk("rv", c, 4 + 2 * c)
                for c in range(2):
                    chunk("gate_r", c, 8 + 2 * c)
                pe.wait_ge(rows_ready, events(1, l, ROWS, 1))
                transposed("rqkT", R["qk"], 8)
                for i in range(4):
                    bank, filled = fill(1, l, "decay", i)
                    turned(1, l, "rqkT", i // 2)
                    turned(1, l, "rqkT", 2 + i // 2)
                    nc.tensor.matmul(bank[:, 0:2 * P], R["qT"][:, 4 + i, 0:P], R["qT"][:, i, :], start=True, stop=True)
                    nc.tensor.matmul(bank[:, 2 * P:3 * P], R["qT"][:, 4 + i, P:2 * P], R["qT"][:, i, P:2 * P],
                                     start=True, stop=True).then_inc(filled, 1)
                for c in range(2):
                    chunk("rg", c, 12 + 2 * c)
                for i in range(4):
                    r, hp = divmod(i, 2)
                    bank, filled = fill(1, l, "ret", i)
                    for s in range(2):
                        hd = 2 * hp + s
                        turned(1, l, "decay", hd)
                        v = slice(hd * 256, hd * 256 + 256)
                        last = nc.tensor.matmul(bank[:, s * 256:(s + 1) * 256], R["w"][:, hd, r * P:(r + 1) * P],
                                                R["v"][:, 0, v], start=True, stop=not r)
                        if r:
                            last = nc.tensor.matmul(bank[:, s * 256:(s + 1) * 256], R["w"][:, hd, 2 * P:3 * P],
                                                    R["v"][:, 1, v], start=False, stop=True)
                    last.then_inc(filled, 1)
                for c in range(2):
                    chunk("aq", c, 16 + 2 * c)
                chunk("akv", 0, 20, cols=256)
                turn(1, l, "turn_r", R["g"], kd, lambda i: pe.wait_ge(ret_ready, l + 1))
                for c in range(2):
                    chunk("br_r", c, 22 + 2 * c, yt, "turn_r" if c == 0 else None)
                pe.wait_ge(rows_ready, events(1, l, ROWS, 2))
                transposed("qkT", B["q"], 8)
                transposed("qkT", B["kk"].rearrange("p r g s n -> p r (g s n)"), 4, 4)
                for i in range(6):
                    turned(1, l, "qkT", i)
                for g in range(2):
                    scores(1, l, g, B["qT"], lambda hp: 4 * g + hp, lambda hp: 8 + 2 * g)
                    project(1, l, f"gate_a{g}", 0, (m + 26 + 2 * g, m + 27 + 2 * g), xt)
                    for r in range(2):
                        probs(1, l, g, r, B["e"], B["pT"], B["v"], lambda hp: g)
                pair, n = chunk_count(1, l, "pv1")
                turn(1, l, "turn_o", B["o"], kd, lambda i: pe.wait_ge(chunk_read[pair], n))
                for c in range(2):
                    chunk("br_a", c, 30 + 2 * c, yt, "turn_o" if c == 0 else None)
                for c in range(3):
                    chunk("xbc", c, 34 + 2 * c)
                pair, n = chunk_count(1, l, "xbc", 2)
                pe.wait_ge(chunk_read[pair], n)
                transposed("xbcT", S["rows"], 12)
                project(1, l, "dt", 0, (m + 40,), xt, 8, 16)
                for c in range(2):
                    chunk("z", c, 41 + 2 * c)
                chunk("gate_s", 0, 45)
                pe.wait_ge(xc_ready, l + 1)
                for i in range(4):
                    r, c = divmod(i, 2)
                    bank, filled = fill(1, l, "xsT", i)
                    for t in range(4):
                        last = nc.tensor.transpose(bank[:, t * P:(t + 1) * P],
                                                   S["conv"][:, 4 * c + t, r * P:(r + 1) * P], ident[:, :])
                    last.then_inc(filled, 1)
                chunk("gate_s", 1, 47)
                for g in range(2):
                    b, c = S["conv"][:, 8 + g, :], S["conv"][:, 10 + g, :]
                    bank, filled = fill(1, l, "cb", g)
                    nc.tensor.matmul(bank[:, 0:2 * P], b[:, 0:P], c, start=True, stop=True)
                    nc.tensor.matmul(bank[:, 2 * P:3 * P], b[:, P:2 * P], c[:, P:2 * P], start=True, stop=True) \
                        .then_inc(filled, 1)
                pe.wait_ge(da_ready, l + 1)
                bank, filled = fill(1, l, "acs")
                nc.tensor.matmul(bank[:, 0:16], causal[:, 0:P], da[:, 0, :], start=True, stop=True)
                nc.tensor.matmul(bank[:, 16:32], causal[:, P:2 * P], da[:, 0, :], start=True, stop=False)
                nc.tensor.matmul(bank[:, 16:32], causal[:, 0:P], da[:, 1, :], start=False, stop=True).then_inc(filled, 1)

                def weigh(hd):
                    pair, n = count("chunks", 1, l, "ys", hd // 8)
                    if hd % 8 == 0:
                        pe.wait_ge(chunk_read[pair], n * 2)
                    pe.wait_ge(seg_ready, l * 16 + (hd + 1))
                    c, v = (hd % 8) * 64, slice(hd * 64, hd * 64 + 64)
                    w = S["seg"][:, hd % 8, :]
                    nc.tensor.matmul(acc[2 * pair][:, c:c + 64], w[:, 0:P], S["xdt"][:, 0, v], start=True, stop=True)
                    nc.tensor.matmul(acc[2 * pair + 1][:, c:c + 64], w[:, P:2 * P], S["xdt"][:, 0, v], start=True,
                                     stop=False)
                    nc.tensor.matmul(acc[2 * pair + 1][:, c:c + 64], w[:, 2 * P:3 * P], S["xdt"][:, 1, v],
                                     start=False, stop=True).then_inc(y_done, 1)

                for hd in range(16):
                    bank, filled = fill(1, l, "seg", hd)
                    wide = lambda r: da[:, r, hd:hd + 1].broadcast_to([P, P])
                    nc.tensor.matmul(bank[:, 0:2 * P], wide(0), causal[:, :], start=True, stop=False)
                    nc.tensor.matmul(bank[:, P:2 * P], wide(1), causal[:, 0:P], start=False, stop=True) \
                        .then_inc(filled, 1)
                    if hd >= 3:
                        weigh(hd - 3)
                for hd in (13, 14, 15):
                    weigh(hd)
                turn(1, l, "turn_s", S["y"], kd, lambda i: pe.wait_ge(y_ready, 2 * l + (1 + i // 2)))
                for c in range(2):
                    chunk("br_s", c, 49 + 2 * c, yt, "turn_s" if c == 0 else None)
                turn_mixed(1, l, mixed2)
                for c in range(2):
                    project_out(1, l, c, (m + 53 + 2 * c, m + 54 + 2 * c), "turn_y" if c == 0 else None)

            for block in range(2):
                with pe.Fori(0, depth) as l:
                    ffn(block, "f1", l)
                    (mixer2 if block else mixer1)(l)
                    ffn(block, "f2", l)

        @block_.scalar
        def _(act):
            def split(block, l, pos, j=0):
                slot, n = unit_count(block, l, pos)
                act.wait_ge(raw_loaded[slot], (n + j) * 32)
                act.wait_ge(unit_used[slot], (n + j) * 2)
                nc.scalar.copy(w_hi[:, slot, :], raw[:, slot, :]).then_inc(hi_split[slot], 1)

            def turn_hi(block, l, name, kts, dst, k0, scale):
                for i in range(kts // 2):
                    bank, n = count("work", block, l, name, i)
                    act.wait_ge(work_filled[bank], n)
                    for t in range(2):
                        s = vec[:, scale[2 * i + t]:scale[2 * i + t] + 1] if isinstance(scale, list) else scale
                        last = nc.scalar.activation(dst[:, k0 + 2 * i + t, :], work[bank][:, t * 256:(t + 1) * 256],
                                                    ACT.Copy, scale=s)
                    last.then_inc(hi_turned, 1)

            def squares(src, to=junk):
                for r in range(2):
                    last = nc.scalar.activation(to[:, r * dm:(r + 1) * dm], src[:, r, :], ACT.Square, accum_out=sq[:, r:r + 1])
                last.then_inc(squared, 1)

            def squares_out(l, name):
                for r in range(2):
                    for c in range(2):
                        i = 2 * r + c
                        act.wait_ge(post_scaled, l * (4 * STAGES) + (4 * stage_of(1, name) + i + 1))
                        last = nc.scalar.activation(junk[:, i * half:(i + 1) * half], acc[i][:, :], ACT.Square,
                                                    accum_out=sq[:, i:i + 1])
                last.then_inc(squared, 1)

            for pos in range(2):
                split(0, 0, pos)
            act.wait_ge(table_ready, 2)
            act.wait_ge(raw_loaded[2], 32)
            act.dma_start(a["scratch"], field[0:16, 5000:5384].unsqueeze(1).broadcast_to([16, P, 3 * P])) \
                .then_inc(scratch_stored, 16)

            def ffn(block, name, l):
                u = first_unit[block, name]
                steps_before = ffn_count(block, l, name, steps)
                if name == "f1":
                    act.wait_ge(gain1_loaded, l * 16 + (16 + 16 * depth * block))
                turn_hi(block, l, "turn_" + name, kd, xt_hi, 0, [gain(name) + t for t in range(kd)])
                squares(h)

                def silu(pos, j, first=False):
                    if first:
                        act.wait_ge(rs_ready, norm_count(block, l, name))
                    for r in range(2):
                        slot, n = used_count(block, l, pos, r, j)
                        act.wait_ge(unit_used[slot], n)
                        nc.scalar.activation(act_gate[:, r, :], work[2 + r][:, 0:NARROW], ACT.Silu,
                                             scale=rs[:, r:r + 1]).then_inc(silu_ready, 1)

                def hidden_halves(step):
                    act.wait_ge(hidden_turned, steps_before + (step + 1))
                    nc.scalar.copy(yt_hi[:, 0:2, :], work[0][:, :].rearrange("p (t n) -> p t n", t=2)) \
                        .then_inc(hidden_hi, 1)

                def step(j):
                    hidden_halves(j)
                    split(block, l, u + 4, j)
                    split(block, l, u + 5, j)
                    silu(u + 3, j)
                    split(block, l, u + 6, j)

                split(block, l, u + 2)
                split(block, l, u + 3)
                silu(u + 1, 0, True)
                with act.Fori(0, steps - 2) as j:
                    step(j)
                step(steps - 2)
                hidden_halves(steps - 1)
                split(block, l, u + 3 * steps + 1)
                if block:
                    squares_out(l, name)

            def take(block, l, name, i, pos, parts, func=ACT.Copy):
                pair, _ = count("chunks", block, l, name, i)
                for r in range(2):
                    slot, n = used_count(block, l, pos, r)
                    act.wait_ge(unit_used[slot], n)
                    for cols, dst in parts:
                        last = nc.scalar.activation(dst(r), acc[2 * pair + r][:, cols], func, scale=rs[:, r:r + 1])
                    last.then_inc(chunk_read[pair], 1)

            def copy_bank(block, l, name, i, dst):
                bank, n = count("work", block, l, name, i)
                act.wait_ge(work_filled[bank], n)
                nc.scalar.copy(dst, work[bank][:, :].rearrange("p (t n) -> p t n", t=2)).then_inc(work_read[bank], 1)

            def gate(block, l, name, i, g, k):
                pair, _ = count("chunks", block, l, name, i)
                for r in range(2):
                    act.wait_ge(chunk_read[pair], chunk_count(block, l, name, i, r)[1])
                    nc.scalar.activation(g[:, r, :], g[:, r, :], ACT.Tanh, scale=0.5).then_inc(gate_ready, 1)

            def softmax(block, l, g, e, then):
                for r in range(2):
                    cols = P * key_tiles(block, r)
                    act.wait_ge(tops_ready, events(block, l, [2 * n for n in PASSES], 2 * g + r + 1))
                    nc.scalar.activation(sink_e[:, r, :], sink_e[:, r, :], ACT.Exp)
                    for i in range(8):
                        piece = e(4 * r + i // 2)[:, i % 2, 0:cols]
                        last = nc.scalar.activation(piece, piece, ACT.Exp, bias=minus_top[:, r, i:i + 1],
                                                    accum_out=total[:, r, i:i + 1])
                        if i % 2:
                            last.then_inc(probs_ready, 1)
                    then()

            def mixer1(l):
                m = first_unit[0, "m"]
                up = iter(range(m + 2, m + 23))
                ahead = lambda n: [split(0, l, next(up)) for _ in range(n)]
                act.wait_ge(vec_loaded, l * 32 + 32)
                turn_hi(0, l, "turn_m", kd, xt_hi, 0, [gain("m") + t for t in range(kd)])
                squares(h)
                act.wait_ge(scratch_stored, 16)
                ahead(2)
                act.wait_ge(rs_ready, norm_count(0, l, "m"))
                take(0, l, "q", 0, m + 1, [(slice(0, 512), lambda r: A["qk"][:, r, 0:512])])
                ahead(1)
                take(0, l, "kv", 0, m + 2, [(slice(0, P), lambda r: A["qk"][:, r, 512:640]),
                                            (slice(P, 2 * P), lambda r: A["v"][:, r, :])])
                ahead(2)
                take(0, l, "p", 0, m + 4, [(slice(0, 512), lambda r: A["p"][:, r, :])])
                ahead(2)
                gate(0, l, "gate", 0, A["gate"][0][:, :, 0:512], 0)
                for i in range(2):
                    copy_bank(0, l, "pool", i, A["pooled"][:, 2 * i:2 * i + 2, :])
                for i in range(4):
                    copy_bank(0, l, "qkT", i, A["qT"][:, 2 * i:2 * i + 2, :])
                ahead(2)
                gate(0, l, "gate", 1, A["gate"][0][:, :, 512:1024], 1)
                softmax(0, l, 0, A["e"], lambda: ahead(1))
                gate(0, l, "gate", 2, A["gate"][1][:, :, 0:512], 2)
                ahead(2)
                gate(0, l, "gate_b", 0, A["gate"][1][:, :, 512:1024], 3)
                turn_hi(0, l, "mixp", 4, yt_hi, 4, [24 + t for t in range(4)])
                turn_hi(0, l, "turn_o", 4, yt_hi, 0, 1.0)
                ahead(4)
                turn_hi(0, l, "turn_y", kd, yt_hi, 0, 0.5)
                ahead(4)

            def mixer2(l):
                m = first_unit[1, "m"]
                up = iter(range(m + 2, m + 59))
                ahead = lambda n: [split(1, l, next(up)) for _ in range(n)]

                def rows(name, c, last, dst, func=ACT.Copy):
                    take(1, l, name, c, m + last, [(slice(0, 512), lambda r: dst[:, r, c * 512:(c + 1) * 512])], func)

                act.wait_ge(vec_loaded, l * 32 + (32 + 32 * depth))
                turn_hi(1, l, "turn_m", kd, xt_hi, 0, [gain("m") + t for t in range(kd)])
                squares(h)
                ahead(2)
                act.wait_ge(rs_ready, norm_count(1, l, "m"))
                rows("rqk", 0, 1, R["qk"])
                ahead(2)
                rows("rqk", 1, 3, R["qk"])
                ahead(2)
                rows("rv", 0, 5, R["v"])
                ahead(2)
                rows("rv", 1, 7, R["v"])
                ahead(2)
                gate(1, l, "gate_r", 0, mixed2[:, :, 0:512], 0)
                ahead(2)
                gate(1, l, "gate_r", 1, mixed2[:, :, 512:1024], 1)
                for i in range(4):
                    copy_bank(1, l, "rqkT", i, R["qT"][:, 2 * i:2 * i + 2, :])
                ahead(2)
                rows("rg", 0, 13, R["g"], ACT.Silu)
                ahead(2)
                rows("rg", 1, 15, R["g"], ACT.Silu)
                ahead(2)
                rows("aq", 0, 17, B["q"])
                ahead(2)
                rows("aq", 1, 19, B["q"])
                ahead(1)
                take(1, l, "akv", 0, m + 21, [(slice(0, P), lambda r: B["k"][:, r, :]),
                                              (slice(P, 2 * P), lambda r: B["v"][:, r, :])])
                ahead(1)
                turn_hi(1, l, "turn_r", kd, yt_hi, 0, [gain("ret") + t for t in range(kd)])
                ahead(4)
                for i in range(6):
                    copy_bank(1, l, "qkT", i, B["qT"][:, 2 * i:2 * i + 2, :])
                for g in range(2):
                    softmax(1, l, g, B["e"], lambda: ahead(1))
                    gate(1, l, f"gate_a{g}", 0, B["gate"][:, :, g * 512:(g + 1) * 512], 4 + 2 * g)
                turn_hi(1, l, "turn_o", kd, yt_hi, 0, 1.0)
                ahead(6)
                for c in range(3):
                    rows("xbc", c, 35 + 2 * c, S["rows"])
                    ahead(2 if c < 2 else 1)
                act.wait_ge(padded_ready, l + 1)
                for i in range(6):
                    copy_bank(1, l, "xbcT", i, S["padded"][:, 2 * i:2 * i + 2, 3:2 * P + 3])
                ahead(3)
                rows("z", 0, 42, S["z"], ACT.Silu)
                rows("z", 1, 44, S["z"], ACT.Silu)
                ahead(2)
                act.wait_ge(dt_abs_ready, l + 1)
                nc.scalar.activation(dt_e[:, :, :], dt_abs[:, :, :], ACT.Exp, scale=-1.0)
                nc.scalar.activation(a_exp, row[:, 16:32], ACT.Exp).then_inc(dt_exp_ready, 1)
                act.wait_ge(conv_ready, l + 1)
                for t in range(12):
                    last = nc.scalar.activation(S["conv"][:, t, :], S["conv"][:, t, :], ACT.Silu,
                                                bias=vec[:, 40 + t:41 + t])
                last.then_inc(xc_ready, 1)
                ahead(2)
                gate(1, l, "gate_s", 0, S["gate"][:, :, 0:512], 8)
                ahead(2)
                gate(1, l, "gate_s", 1, S["gate"][:, :, 512:1024], 10)
                for hd in range(16):
                    bank, n = count("work", 1, l, "seg", hd)
                    act.wait_ge(work_read[bank], n + 1)
                    w = S["seg"][:, hd % 8, :]
                    nc.scalar.activation(w, w, ACT.Exp).then_inc(seg_exp, 1)
                act.wait_ge(y_ready, 2 * l + 2)
                squares(S["y"], field[:, 11300:12324].bitcast(mybir.dt.bfloat16))
                turn_hi(1, l, "turn_s", kd, yt_hi, 0, [gain("s") + t for t in range(kd)])
                ahead(4)
                turn_hi(1, l, "turn_y", kd, yt_hi, 0, 0.5)
                ahead(3)
                squares_out(l, "m")

            for block in range(2):
                with act.Fori(0, depth) as l:
                    ffn(block, "f1", l)
                    (mixer2 if block else mixer1)(l)
                    ffn(block, "f2", l)
                if not block:
                    act.wait_ge(h_ready, h_count(0, 0, STAGES * depth))
                    squares(h)

        @block_.vector
        def _(dve):
            for s in range(SLOTS):
                dve.sem_inc(unit_split[s], 1)
            for i in range(4):
                dve.sem_inc(work_read[i], 1)
            for i in range(2):
                dve.sem_inc(chunk_read[i], 2)
            dve.wait_ge(table_ready, 1)
            dve.wait_ge(consts_loaded, 96)
            nc.vector.tensor_tensor(field[0:16, 5000:5384], acc[0][0:16, 0:3 * P], field[0:16, 4600:4984], ALU.add) \
                .then_inc(table_ready, 1)
            dve.wait_ge(x_loaded, 16)
            for r in range(2):
                for c in range(2):
                    nc.vector.tensor_copy(h[:, r, c * half:(c + 1) * half],
                                          field[:, (2 * r + c) * half:(2 * r + c + 1) * half]).then_inc(h_ready, 1)

            def split(block, l, pos, j=0):
                slot, n = unit_count(block, l, pos)
                dve.wait_ge(hi_split[slot], n + j)
                nc.vector.tensor_tensor(w_lo[:, slot, :], raw[:, slot, :], w_hi[:, slot, :].bitcast(F32),
                                        ALU.subtract).then_inc(unit_split[slot], 1)

            def turn_lo(block, l, name, kts, hi, lo, k0, scale):
                for i in range(kts // 2):
                    bank, _ = count("work", block, l, name, i)
                    dve.wait_ge(hi_turned, count("split", block, l, name, i)[1])
                    for t in range(2):
                        k = 2 * i + t
                        s = vec[:, scale[k]:scale[k] + 1] if isinstance(scale, list) else scale
                        last = nc.vector.scalar_tensor_tensor(
                            lo[:, k0 + k, :], work[bank][:, t * 256:(t + 1) * 256], s,
                            hi[:, k0 + k, :].bitcast(F32), ALU.mult, ALU.subtract)
                    last.then_inc(work_read[bank], 1)

            def mean(n, parts=1):
                dve.wait_ge(squared, n)
                if parts == 2:
                    q = sq[:, 0:4].rearrange("p (r c) -> p r c", r=2)
                    nc.vector.tensor_tensor(ms[:, :], q[:, :, 0], q[:, :, 1], ALU.add).then_inc(pair_added, 1)
                    dve.wait_ge(pair_added, 1)
                    dve.sem_clear(pair_added)
                nc.vector.tensor_scalar(ms[:, :], ms[:, :] if parts == 2 else sq[:, 0:2], 1.0 / dm, EPS,
                                        ALU.mult, ALU.add).then_inc(mean_ready, 1)

            def ffn(block, name, l):
                u = first_unit[block, name]
                steps_before = ffn_count(block, l, name, steps)
                silus_before = ffn_count(block, l, name, 2 * steps)
                if name == "f1":
                    dve.wait_ge(gain1_loaded, l * 16 + (16 + 16 * depth * block))
                turn_lo(block, l, "turn_" + name, kd, xt_hi, xt_lo, 0, [gain(name) + t for t in range(kd)])
                mean(norm_count(block, l, name))

                def hidden(s, first=False):
                    if first:
                        dve.wait_ge(rs_ready, norm_count(block, l, name))
                    for r in range(2):
                        dve.wait_ge(silu_ready, silus_before + (s * 2 + (r + 1)))
                        nc.vector.scalar_tensor_tensor(hid[:, r, :], work[2 + r][:, NARROW:2 * NARROW],
                                                       rs[:, r:r + 1], act_gate[:, r, :], ALU.mult, ALU.mult) \
                            .then_inc(hidden_ready, 1)

                def hidden_halves(s):
                    dve.wait_ge(hidden_hi, steps_before + (s + 1))
                    nc.vector.tensor_tensor(yt_lo[:, 0:2, :], work[0][:, :].rearrange("p (t n) -> p t n", t=2),
                                            yt_hi[:, 0:2, :].bitcast(F32), ALU.subtract).then_inc(hidden_split, 1)

                def step(j):
                    hidden_halves(j)
                    split(block, l, u + 4, j)
                    split(block, l, u + 5, j)
                    hidden(j + 1)
                    split(block, l, u + 6, j)

                split(block, l, u + 2)
                split(block, l, u + 3)
                hidden(0, True)
                with dve.Fori(0, steps - 2) as j:
                    step(j)
                step(steps - 2)
                hidden_halves(steps - 1)
                split(block, l, u + 3 * steps + 1)
                if block:
                    add_normed(block, l, name, 0.5, [acc[i] for i in range(4)])
                else:
                    for r in range(2):
                        slot, n = used_count(block, l, u + 3 * steps - 1, r)
                        dve.wait_ge(unit_used[slot], n)
                        for c in range(2):
                            hh = h[:, r, c * half:(c + 1) * half]
                            nc.vector.scalar_tensor_tensor(hh, acc[2 * r + c][:, :], 0.5, hh, ALU.mult, ALU.add) \
                                .then_inc(h_ready, 1)

            def add_normed(block, l, name, by, banks):
                n = norm_count(block, l, "p" + {"f1": "1", "f2": "2", "m": "m"}[name])
                last_unit = first_unit[1, "m"] + 56 if name == "m" else first_unit[1, name] + 3 * steps - 1
                dve.wait_ge(post_loaded, l * (16 * STAGES) + (16 + 16 * (stage_of(block, name) + 1)))
                for i, bank in enumerate(banks):
                    slot, used = used_count(block, l, last_unit, i // 2)
                    dve.wait_ge(unit_used[slot], used)
                    nc.vector.scalar_tensor_tensor(tmp[:, i, :], bank[:, :], by, post[:, (i % 2) * half:(i % 2 + 1) * half],
                                                   ALU.mult, ALU.mult).then_inc(post_scaled, 1)
                mean(n, 2)
                dve.wait_ge(rs_ready, n)
                dve.wait_ge(post_scaled, l * (4 * STAGES) + (4 * stage_of(block, name) + 4))
                for i in (0, 2, 1, 3):
                    hh = h[:, i // 2, (i % 2) * half:(i % 2 + 1) * half]
                    nc.vector.scalar_tensor_tensor(hh, tmp[:, i, :], rp[:, i // 2:i // 2 + 1], hh, ALU.mult, ALU.add) \
                        .then_inc(h_ready, 1)

            done = [0]

            def mark(ins):
                ins.then_inc(dve_step, 1)
                done[0] += 1

            def settle():
                dve.wait_ge(dve_step, done[0])

            def add_bias(block, l, name, i, pos, g, slot_, c):
                pair, _ = count("chunks", block, l, name, i)
                for r in range(2):
                    slot, n = used_count(block, l, pos, r)
                    dve.wait_ge(unit_used[slot], n)
                    nc.vector.scalar_tensor_tensor(g[:, r, :], acc[2 * pair + r][:, :], rs[:, r:r + 1],
                                                   bias[:, slot_, c * half:(c + 1) * half], ALU.mult, ALU.add) \
                        .then_inc(chunk_read[pair], 1)

            def place_k(kk, k):
                for r in range(2):
                    for s in range(2):
                        last = nc.vector.tensor_copy(kk[:, r, :, s, 64 * s:64 * s + 64],
                                                     k(r).rearrange("p (g d) -> p g d", g=2))
                return last

            def mask_scores(block, l, g, e, by_head, sink):
                for r in range(2):
                    cols = P * key_tiles(block, r)
                    for hp in range(4):
                        bank, n = count("work", block, l, f"scores{g}", 4 * r + hp)
                        dve.wait_ge(work_filled[bank], n)
                        piece = e(4 * r + hp)[:, :, 0:cols]
                        nc.vector.scalar_tensor_tensor(
                            piece, work[bank][:, :].rearrange("p (s n) -> p s n", s=2)[:, :, 0:cols], 64 ** -0.5,
                            by_head(r, hp), ALU.mult, ALU.add).then_inc(work_read[bank], 1)
                        dve.wait_ge(work_read[bank], n + 1)
                        mark(nc.vector.tensor_reduce(top[:, r, 2 * hp:2 * hp + 2], piece, AX.X, ALU.max))
                    settle()
                    mark(nc.vector.tensor_tensor(top[:, r, :], top[:, r, :], sink, ALU.max))
                    settle()
                    mark(nc.vector.tensor_scalar(minus_top[:, r, :], top[:, r, :], -1.0, None, ALU.mult))
                    settle()
                    nc.vector.tensor_tensor(sink_e[:, r, :], sink, top[:, r, :], ALU.subtract).then_inc(tops_ready, 1)

            def take_probs(block, l, g, r, pT, o, between=None):
                passes = [8 * n for n in PASSES]
                nk = key_tiles(block, r)
                for i in range(4 * r, 4 * r + 4):
                    bank, n = count("work", block, l, f"probsT{g}", i)
                    dve.wait_ge(work_filled[bank], n)
                    if i >= 2:
                        dve.wait_ge(pv_done, events(block, l, passes, 8 * g + i - 1))
                    nc.vector.tensor_copy(pT[:, i % 2, 0:2 * nk * P], work[bank][:, 0:2 * nk * P]) \
                        .then_inc(work_read[bank], 1)
                    if between and i % 4 == 1:
                        between()
                mark(nc.vector.tensor_tensor(total[:, r, :], total[:, r, :], sink_e[:, r, :], ALU.add))
                settle()
                mark(nc.vector.reciprocal(inv[:, r, :], total[:, r, :]))
                settle()
                pair, _ = count("chunks", block, l, f"pv{g}")
                dve.wait_ge(pv_done, events(block, l, passes, 8 * g + 4 * r + 4))
                nc.vector.tensor_tensor(o[:, r, g * 512:(g + 1) * 512].rearrange("p (h d) -> p h d", h=8),
                                        acc[2 * pair + r][:, :].rearrange("p (h d) -> p h d", h=8),
                                        inv[:, r, :].unsqueeze(2).broadcast_to([P, 8, 64]), ALU.mult) \
                    .then_inc(chunk_read[pair], 1)

            def gated(block, l, name, c, pos, g, k):
                pair, _ = count("chunks", block, l, name, c)
                dve.wait_ge(gate_ready, events(block, l, GATES, k))
                for r in range(2):
                    slot, n = used_count(block, l, pos, r)
                    dve.wait_ge(unit_used[slot], n)
                    gg = g[:, r, c * half:(c + 1) * half]
                    nc.vector.scalar_tensor_tensor(gg, gg, 1.0, acc[2 * pair + r][:, :], ALU.add, ALU.mult) \
                        .then_inc(chunk_read[pair], 1)

            def mixer1(l):
                m = first_unit[0, "m"]
                dve.sem_clear(dve_step)
                done[0] = 0
                up = iter(range(m + 2, m + 23))
                ahead = lambda n: [split(0, l, next(up)) for _ in range(n)]
                dve.wait_ge(vec_loaded, l * 32 + 32)
                turn_lo(0, l, "turn_m", kd, xt_hi, xt_lo, 0, [gain("m") + t for t in range(kd)])
                mean(norm_count(0, l, "m"))
                ahead(3)
                pair, n = chunk_count(0, l, "kv")
                dve.wait_ge(chunk_read[pair], n)
                mark(nc.vector.memset(A["kk"], 0.0))
                heads = [A["qk"][:, r, :].rearrange("p (h d) -> p h d", d=64) for r in range(2)]
                part = lambda r, i: A["rope"][:, r, i, :].rearrange("p (h d) -> p h d", d=16)
                wide = lambda r, i, c0, c1: rope1[:, r, i, c0:c1].unsqueeze(1).broadcast_to([P, 10, c1 - c0])
                for r in range(2):
                    x, a_, b_ = heads[r], part(r, 0), part(r, 1)
                    mark(nc.vector.tensor_tensor(a_, x[:, :, 0:16], wide(r, 0, 0, 16), ALU.mult))
                    mark(nc.vector.tensor_tensor(b_[:, :, 0:8], x[:, :, 8:16], wide(r, 1, 0, 8), ALU.mult))
                    mark(nc.vector.tensor_tensor(b_[:, :, 8:16], x[:, :, 0:8], wide(r, 1, 8, 16), ALU.mult))
                settle()
                for r in range(2):
                    mark(nc.vector.tensor_tensor(heads[r][:, :, 0:16], part(r, 0), part(r, 1), ALU.add))
                settle()
                place_k(A["kk"], lambda r: A["qk"][:, r, 512:640]).then_inc(rows_ready, 1)
                ahead(4)
                dve.wait_ge(bias_loaded[0], events(0, l, (16, 32), 16))
                add_bias(0, l, "gate", 0, m + 6, A["gate"][0][:, :, 0:512], 0, 0)
                ahead(2)
                add_bias(0, l, "gate", 1, m + 8, A["gate"][0][:, :, 512:1024], 0, 1)
                dve.wait_ge(blk_loaded, events(0, l, (48, 48), 48))
                mask_scores(0, l, 0, A["e"], lambda r, hp: band[:, r, :].unsqueeze(1).broadcast_to([P, 2, 256]),
                            row[:, 0:8])
                ahead(1)
                take_probs(0, l, 0, 0, A["pT"], A["o"], lambda: ahead(1))
                dve.wait_ge(bias_loaded[1], events(0, l, (16, 16), 16))
                add_bias(0, l, "gate", 2, m + 10, A["gate"][1][:, :, 0:512], 1, 0)
                ahead(2)
                add_bias(0, l, "gate_b", 0, m + 12, A["gate"][1][:, :, 512:1024], 1, 1)
                take_probs(0, l, 0, 1, A["pT"], A["o"])
                turn_lo(0, l, "mixp", 4, yt_hi, yt_lo, 4, [24 + t for t in range(4)])
                turn_lo(0, l, "turn_o", 4, yt_hi, yt_lo, 0, 1.0)
                ahead(2)
                for c in range(2):
                    gated(0, l, "br_a", c, m + 13 + c, A["gate"][0], 2 * c + 2)
                ahead(2)
                for c in range(2):
                    gated(0, l, "br_p", c, m + 15 + c, A["gate"][1], 2 * c + 6)
                for c in range(2):
                    pair, n = chunk_count(0, l, "br_p", c)
                    dve.wait_ge(chunk_read[pair], n)
                    for r in range(2):
                        g = [A["gate"][i][:, r, c * half:(c + 1) * half] for i in range(2)]
                        nc.vector.tensor_tensor(g[0], g[0], g[1], ALU.add).then_inc(mixed_ready, 1)
                turn_lo(0, l, "turn_y", kd, yt_hi, yt_lo, 0, 0.5)
                ahead(2)
                for c in range(2):
                    for r in range(2):
                        slot, n = used_count(0, l, m + 18 + 2 * c, r)
                        dve.wait_ge(unit_used[slot], n)
                        hh = h[:, r, c * half:(c + 1) * half]
                        nc.vector.tensor_tensor(hh, acc[2 * r + c][:, :], hh, ALU.add).then_inc(h_ready, 1)
                    if c == 0:
                        ahead(2)

            def mixer2(l):
                m = first_unit[1, "m"]
                dve.sem_clear(dve_step)
                done[0] = 0
                up = iter(range(m + 2, m + 59))
                ahead = lambda n: [split(1, l, next(up)) for _ in range(n)]
                tt, stt, ts = nc.vector.tensor_tensor, nc.vector.scalar_tensor_tensor, nc.vector.tensor_scalar
                dve.wait_ge(vec_loaded, l * 32 + (32 + 32 * depth))
                turn_lo(1, l, "turn_m", kd, xt_hi, xt_lo, 0, [gain("m") + t for t in range(kd)])
                mean(norm_count(1, l, "m"))
                ahead(6)
                dve.wait_ge(blk_loaded, 48 * depth + 48)
                pair, n = chunk_count(1, l, "rqk", 1)
                dve.wait_ge(chunk_read[pair], n)
                pair, n = chunk_count(1, l, "rqk", 0)
                dve.wait_ge(chunk_read[pair], n)
                for r in range(2):
                    x = R["qk"][:, r, :].rearrange("p (h d) -> p h d", h=8)
                    a_, b_ = R["rope"]
                    wide = lambda i, c0, c1: rope2[:, r, i, c0:c1].unsqueeze(1).broadcast_to([P, 8, c1 - c0])
                    mark(tt(a_, x, wide(0, 0, P), ALU.mult))
                    mark(tt(b_[:, :, 0:64], x[:, :, 64:P], wide(1, 0, 64), ALU.mult))
                    mark(tt(b_[:, :, 64:P], x[:, :, 0:64], wide(1, 64, P), ALU.mult))
                    settle()
                    last = tt(x, a_, b_, ALU.add)
                    if not r:
                        mark(last)
                        settle()
                last.then_inc(rows_ready, 1)
                ahead(4)
                dve.wait_ge(bias_loaded[0], events(1, l, (16, 32), 16))
                add_bias(1, l, "gate_r", 0, m + 9, mixed2[:, :, 0:512], 0, 0)
                ahead(2)
                add_bias(1, l, "gate_r", 1, m + 11, mixed2[:, :, 512:1024], 0, 1)
                for i in range(4):
                    bank, n = count("work", 1, l, "decay", i)
                    dve.wait_ge(work_filled[bank], n)
                    tt(R["w"][:, i, 0:2 * P], work[bank][:, 0:2 * P], decay[:, i, :], ALU.mult)
                    tt(R["w"][:, i, 2 * P:3 * P], work[bank][:, 2 * P:3 * P], decay[:, i, 0:P], ALU.mult) \
                        .then_inc(work_read[bank], 1)
                ahead(4)
                for c in range(2):
                    pair, n = chunk_count(1, l, "rg", c)
                    dve.wait_ge(chunk_read[pair], n)
                for i in range(4):
                    r, hp = divmod(i, 2)
                    bank, n = count("work", 1, l, "ret", i)
                    dve.wait_ge(work_filled[bank], n)
                    for s in range(2):
                        mark(nc.vector.bn_stats(bn[:, 2 * i + s, :], work[bank][:, s * 256:(s + 1) * 256]))
                    settle()
                    for s in range(2):
                        mark(nc.vector.bn_aggr(mv[:, 2 * i + s, :], bn[:, 2 * i + s, :]))
                    settle()
                    for s in range(2):
                        g = R["g"][:, r, (2 * hp + s) * 256:(2 * hp + s + 1) * 256]
                        last = stt(g, work[bank][:, s * 256:(s + 1) * 256], mv[:, 2 * i + s, 0:1], g, ALU.subtract,
                                   ALU.mult)
                    last.then_inc(work_read[bank], 1)
                ts(ret_var, mv[:, :, 1], EPS, None, ALU.add).then_inc(ret_var_ready, 1)
                ahead(2)
                dve.wait_ge(ret_rstd_ready, l + 1)
                for i in range(4):
                    bank, n = count("work", 1, l, "ret", i)
                    dve.wait_ge(work_read[bank], n + 1)
                for r in range(2):
                    g = R["g"][:, r, :].rearrange("p (h d) -> p h d", h=4)
                    last = tt(g, g, ret_rstd[:, 4 * r:4 * r + 4].unsqueeze(2).broadcast_to([P, 4, 256]), ALU.mult)
                last.then_inc(ret_ready, 1)
                ahead(3)
                pair, n = chunk_count(1, l, "akv")
                dve.wait_ge(chunk_read[pair], n)
                mark(nc.vector.memset(B["kk"], 0.0))
                settle()
                place_k(B["kk"], lambda r: B["k"][:, r, :]).then_inc(rows_ready, 1)
                ahead(1)
                turn_lo(1, l, "turn_r", kd, yt_hi, yt_lo, 0, [gain("ret") + t for t in range(kd)])
                ahead(2)
                gated(1, l, "br_r", 0, m + 23, mixed2, 2)
                ahead(2)
                gated(1, l, "br_r", 1, m + 25, mixed2, 4)
                for g in range(2):
                    mask_scores(1, l, g, B["e"], lambda r, hp: rel_bias[:, 8 * g + 2 * hp:8 * g + 2 * hp + 2,
                                                                       (0 if r else P):2 * P],
                                row[:, 48 + 8 * g:56 + 8 * g])
                    ahead(1)
                    take_probs(1, l, g, 0, B["pT"], B["o"], lambda: ahead(1))
                    dve.wait_ge(bias_loaded[1], events(1, l, (16, 16), 16))
                    add_bias(1, l, f"gate_a{g}", 0, m + 27 + 2 * g, B["gate"][:, :, g * 512:(g + 1) * 512], 1, g)
                    take_probs(1, l, g, 1, B["pT"], B["o"])
                turn_lo(1, l, "turn_o", kd, yt_hi, yt_lo, 0, 1.0)
                ahead(2)
                gated(1, l, "br_a", 0, m + 31, B["gate"], 6)
                ahead(2)
                gated(1, l, "br_a", 1, m + 33, B["gate"], 8)
                for c in range(2):
                    for name in ("br_r", "br_a"):
                        pair, n = chunk_count(1, l, name, c)
                        dve.wait_ge(chunk_read[pair], n)
                for r in range(2):
                    mark(tt(mixed2[:, r, :], mixed2[:, r, :], B["gate"][:, r, :], ALU.add))
                ahead(6)
                pair, n = chunk_count(1, l, "xbc", 2)
                dve.wait_ge(chunk_read[pair], n)
                nc.vector.memset(S["padded"][:, :, 0:3], 0.0).then_inc(padded_ready, 1)
                ahead(1)
                x, y = S["padded"], S["conv"]
                for i in range(6):
                    bank, n = count("work", 1, l, "xbcT", i)
                    dve.wait_ge(work_read[bank], n + 1)
                for tap in range(4):
                    for t in range(12):
                        w = vec[:, 52 + 12 * tap + t:53 + 12 * tap + t]
                        src = x[:, t, tap:tap + 2 * P]
                        if tap == 0:
                            last = ts(y[:, t, :], src, w, None, ALU.mult)
                        else:
                            last = stt(y[:, t, :], src, w, y[:, t, :], ALU.mult, ALU.add)
                        if tap == 3 and t == 11:
                            last.then_inc(conv_ready, 1)
                        else:
                            mark(last)
                    if tap < 3:
                        settle()
                    ahead(1)
                    if tap == 0:
                        pair, _ = count("chunks", 1, l, "dt")
                        for r in range(2):
                            slot, n = used_count(1, l, m + 40, r)
                            dve.wait_ge(unit_used[slot], n)
                            stt(dt_x[:, r, :], acc[2 * pair + r][:, 0:16], rs[:, r:r + 1], row[:, 0:16], ALU.mult, ALU.add) \
                                .then_inc(chunk_read[pair], 1)
                        dve.wait_ge(chunk_read[pair], chunk_count(1, l, "dt")[1])
                        stt(dt_abs, dt_x, -1.0, dt_x, ALU.mult, ALU.max).then_inc(dt_abs_ready, 1)
                ahead(1)
                dve.wait_ge(dt_exp_ready, l + 1)
                mark(ts(dt_z, dt_e, 2.0, None, ALU.add))
                settle()
                mark(nc.vector.reciprocal(dt_z, dt_z))
                settle()
                mark(tt(dt_z, dt_z, dt_e, ALU.mult))
                settle()
                mark(tt(dt_z2, dt_z, dt_z, ALU.mult))
                settle()
                mark(ts(dt_q, dt_z2, 1.0 / 17, None, ALU.mult))
                settle()
                for k in range(15, 1, -2):
                    mark(stt(dt_q, dt_q, 1.0 / k, dt_z2, ALU.add, ALU.mult))
                    settle()
                mark(stt(dt_q, dt_q, 1.0, dt_z, ALU.add, ALU.mult))
                settle()
                mark(ts(dt, dt_x, 0.0, None, ALU.max))
                settle()
                mark(stt(dt, dt_q, 2.0, dt, ALU.mult, ALU.add))
                settle()
                stt(da, dt, -1.0, a_exp.unsqueeze(1).broadcast_to([P, 2, 16]), ALU.mult, ALU.mult).then_inc(da_ready, 1)
                ahead(2)
                dve.wait_ge(bias_loaded[0], events(1, l, (16, 32), 32))
                add_bias(1, l, "gate_s", 0, m + 46, S["gate"][:, :, 0:512], 0, 0)
                for i in range(4):
                    r, c = divmod(i, 2)
                    bank, n = count("work", 1, l, "xsT", i)
                    dve.wait_ge(work_filled[bank], n)
                    src = work[bank][:, :].rearrange("p (h d) -> p h d", h=8)
                    put = lambda k: S[k][:, r, c * 512:(c + 1) * 512].rearrange("p (h d) -> p h d", h=8)
                    by = lambda v: v.unsqueeze(2).broadcast_to([P, 8, 64])
                    mark(tt(put("xdt"), src, by(dt[:, r, 8 * c:8 * c + 8]), ALU.mult))
                    tt(put("skip"), src, by(row[:, 32 + 8 * c:40 + 8 * c]), ALU.mult).then_inc(work_read[bank], 1)
                ahead(2)
                add_bias(1, l, "gate_s", 1, m + 48, S["gate"][:, :, 512:1024], 0, 1)
                for g in range(2):
                    bank, n = count("work", 1, l, "cb", g)
                    dve.wait_ge(work_filled[bank], n)
                    tt(S["cb"][:, g, 0:2 * P], work[bank][:, 0:2 * P], causal[:, :], ALU.mult)
                    tt(S["cb"][:, g, 2 * P:3 * P], work[bank][:, 2 * P:3 * P], causal[:, 0:P], ALU.mult) \
                        .then_inc(work_read[bank], 1)
                bank, n = count("work", 1, l, "acs")
                dve.wait_ge(work_filled[bank], n)
                nc.vector.tensor_copy(sm[:, 320:352], work[bank][:, 0:32]).then_inc(work_read[bank], 1)
                dve.wait_ge(work_read[bank], n + 1)

                def shift(hd):
                    bank, n = count("work", 1, l, "seg", hd)
                    dve.wait_ge(work_filled[bank], n)
                    if hd >= 8:
                        dve.wait_ge(y_done, l * 16 + (hd - 7))
                    w = S["seg"][:, hd % 8, :]
                    ts(w[:, 0:2 * P], work[bank][:, 0:2 * P], a_cs[:, 0, hd:hd + 1], 0.0, ALU.subtract, ALU.min)
                    ts(w[:, 2 * P:3 * P], work[bank][:, P:2 * P], a_cs[:, 1, hd:hd + 1], 0.0, ALU.subtract,
                       ALU.min).then_inc(work_read[bank], 1)

                def weights(hd):
                    dve.wait_ge(seg_exp, l * 16 + (hd + 1))
                    w = S["seg"][:, hd % 8, :]
                    tt(w, w, S["cb"][:, hd // 8, :], ALU.mult).then_inc(seg_ready, 1)

                def outputs(g):
                    c = slice(g * 512, (g + 1) * 512)
                    pair, n = chunk_count(1, l, "ys", g)
                    dve.wait_ge(y_done, l * 16 + 8 * (g + 1))
                    for r in range(2):
                        tt(S["y"][:, r, c], acc[2 * pair + r][:, :], S["skip"][:, r, c], ALU.add) \
                            .then_inc(chunk_read[pair], 1)
                    dve.wait_ge(chunk_read[pair], n)
                    if not g:
                        for z in range(2):
                            pair, n = chunk_count(1, l, "z", z)
                            dve.wait_ge(chunk_read[pair], n)
                    for r in range(2):
                        last = tt(S["y"][:, r, c], S["y"][:, r, c], S["z"][:, r, c], ALU.mult)
                    last.then_inc(y_ready, 1)

                for hd in range(16):
                    if hd == 13:
                        outputs(0)
                    shift(hd)
                    if hd >= 2:
                        weights(hd - 2)
                weights(14)
                weights(15)
                outputs(1)
                mean(norm_count(1, l, "s"))
                turn_lo(1, l, "turn_s", kd, yt_hi, yt_lo, 0, [gain("s") + t for t in range(kd)])
                ahead(2)
                gs = S["gate"]
                dve.wait_ge(gate_ready, events(1, l, GATES, 12))
                mark(ts(gs, gs, 1.0, None, ALU.add))
                settle()
                dve.wait_ge(rs_ready, norm_count(1, l, "s"))
                for c in range(2):
                    if c:
                        ahead(1)
                    pair, _ = count("chunks", 1, l, "br_s", c)
                    for r in range(2):
                        slot, n = used_count(1, l, m + 50 + 2 * c, r)
                        dve.wait_ge(unit_used[slot], n)
                        gg = gs[:, r, c * half:(c + 1) * half]
                        stt(gg, acc[2 * pair + r][:, :], rp[:, r:r + 1], gg, ALU.mult, ALU.mult) \
                            .then_inc(chunk_read[pair], 1)
                    pair, n = chunk_count(1, l, "br_s", c)
                    dve.wait_ge(chunk_read[pair], n)
                    for r in range(2):
                        g = [x[:, r, c * half:(c + 1) * half] for x in (mixed2, gs)]
                        tt(g[0], g[0], g[1], ALU.add).then_inc(mixed_ready, 1)
                ahead(1)
                turn_lo(1, l, "turn_y", kd, yt_hi, yt_lo, 0, 0.5)
                ahead(3)
                add_normed(1, l, "m", 1.0, [acc[i] for i in range(4)])

            for pos in range(2):
                split(0, 0, pos)
            for block in range(2):
                with dve.Fori(0, depth) as l:
                    ffn(block, "f1", l)
                    (mixer2 if block else mixer1)(l)
                    ffn(block, "f2", l)
                if not block:
                    mean(sum(T[0]["norms"].total) * depth + 1)
                    dve.wait_ge(rs_ready, sum(T[0]["norms"].total) * depth + 1)
                    dve.wait_ge(post_loaded, 16)
                    for i in (0, 2, 1, 3):
                        hh = h[:, i // 2, (i % 2) * half:(i % 2 + 1) * half]
                        nc.vector.scalar_tensor_tensor(hh, hh, rs[:, i // 2:i // 2 + 1],
                                                       post[:, (i % 2) * half:(i % 2 + 1) * half], ALU.mult, ALU.mult) \
                            .then_inc(h_ready, 1)


def constants():
    f = np.float32
    rows = np.arange(2 * P)
    ang = lambda base, n: rows[:, None].astype(f) * (1.0 / (f(base) ** (np.arange(0, n, 2, dtype=f) / f(n))))[None, :]

    def rope(base, n):
        c, s = np.cos(ang(base, n)).astype(f), np.sin(ang(base, n)).astype(f)
        both = np.stack([np.concatenate([c, c], 1), np.concatenate([-s, s], 1)], 1)
        return np.ascontiguousarray(both.reshape(2, P, 2, n).transpose(1, 0, 2, 3), dtype=f)

    band = np.where(np.abs(rows[:, None] - rows[None, :]) <= 128, 0.0, -1e30)
    window = np.zeros((4, 2 * P, 2 * P))
    for g, w in enumerate((2, 4, 8, 16)):
        for t in rows:
            lo, hi = max(t - w // 2, 0), min(t + w // 2, 2 * P)
            window[g, lo:hi, t] = 1.0 / (hi - lo)
            window[g, t, t] -= 1.0
    diff = rows[None, :] - np.arange(P)[:, None]
    decay = np.stack([np.where(diff >= 0, np.exp(np.maximum(diff, 0) * np.log(1.0 - 2.0 ** (-5.0 - i))), 0.0)
                      for i in range(4)]) * P ** -0.5
    dist = 255 - np.arange(3 * P)
    seen = (dist >= 0) & (dist < 128)
    d = np.maximum(dist, 1).astype(f)
    large = np.minimum(16 + (np.log(d / f(16)) / f(np.log(8.0)) * f(16)).astype(np.int32), 31)
    bucket = np.where(dist < 16, dist, large)
    one_hot = np.where(seen[None, :] & (bucket[None, :] == np.arange(32)[:, None]), 1.0, 0.0)
    unseen = np.broadcast_to(np.where(seen, 0.0, -1e30)[None, :], (16, 3 * P))
    c = {
        "ident": np.eye(P), "causal": diff >= 0, "rope1": rope(500000.0, 16), "rope2": rope(10000.0, P),
        "band": band.reshape(2, P, 2 * P).transpose(1, 0, 2),
        "window": window.reshape(4, 2, P, 2 * P).transpose(2, 0, 1, 3),
        "decay": decay.transpose(1, 0, 2), "one_hot": one_hot, "unseen": unseen,
    }
    return {k: np.ascontiguousarray(v, dtype=f) for k, v in c.items()}


def kernel(**inputs):
    import concourse.bacc as bacc
    from concourse.bass_utils import run_bass_kernel_spmd

    x = {k: np.asarray(v) for k, v in inputs.items()}
    depth = x["ffn1_w1"].shape[0]

    def columns(*names):
        out = []
        for n in names:
            v = x[n].reshape(depth, -1, P)
            out.append(np.moveaxis(v, 2, 1))
        return np.ascontiguousarray(np.concatenate(out, axis=2))

    arrays = {n: np.ascontiguousarray(x[n]) for n in (
        "x", "ffn1_w1", "ffn1_w3", "ffn1_w2", "ffn2_w1", "ffn2_w3", "ffn2_w2", "final_norm",
        "w_in", "b_gate", "pool_w", "w_branch_attn", "w_branch_pool", "w_out", "w_in_2", "b_gate_2", "w_out_2",
        "w_branch_2", "rel_bias_2", "w_ffn1_in_2", "w_ffn1_out_2", "w_ffn2_in_2", "w_ffn2_out_2",
        "ffn1_post_g_2", "ffn2_post_g_2", "mix_post_g_2")}
    arrays["vec0"] = columns("mix_norm", "ffn2_norm", "pool_scale")
    arrays["vec1"] = columns("mix_pre_g_2", "ffn2_pre_g_2", "ssd_norm_g_2", "ret_gn_g_2",
                             "conv_b_2", "conv_w_2")
    first = [columns(n) for n in ("ffn1_norm", "ffn1_pre_g_2")]
    arrays["gain1"] = np.concatenate([*first, first[1][-1:]])
    arrays["row0"] = np.ascontiguousarray(x["attn_sink"])
    arrays["row1"] = np.concatenate([x[n] for n in ("dt_bias_2", "a_log_2", "d_skip_2", "attn_sinks_2")], axis=1)
    arrays |= constants()
    nc = bacc.Bacc("TRN2", target_bir_lowering=False, num_devices=1)
    aps = {n: nc.dram_tensor(f"{n}_dram", v.shape, mybir.dt.from_np(v.dtype), kind="ExternalInput").ap()
           for n, v in arrays.items()}
    aps["out"] = nc.dram_tensor("out_dram", x["x"].shape, F32, kind="ExternalOutput").ap()
    aps["scratch"] = nc.dram_tensor("scratch_dram", (16, P, 3 * P), F32, kind="Internal").ap()
    build(nc, aps)
    r = run_bass_kernel_spmd(nc, [{f"{n}_dram": v for n, v in arrays.items()}], core_ids=[0])
    return r.results[0]["out_dram"]
```
